# Optimizing a Trainium2 kernel written in Bass

```python
import jax
import jax.numpy as jnp
from jax import lax
import numpy as np
import math
import jax, jax.numpy as jnp

D_MODEL = 1024
BATCH = 1
SEQ = 256
DEPTH = 1

N_META = 16
CHUNK = 128
PAD_FRONT = CHUNK - N_META
D_MIX = D_MODEL
RET_HEADS = 4
RET_DK = D_MIX // 2 // RET_HEADS
RET_DV = D_MIX // 2 // RET_HEADS
MLSTM_HEADS = 4
MLSTM_DH = D_MIX // 2 // MLSTM_HEADS
CONV_K = 5
N_EXPERTS = 16
EC_CAPACITY = 2
D_FF = 128 * ((8 * D_MODEL // 3 + 127) // 128)
ROPE_BASE = 10000.0
EPS = 1e-6
NEG = -1e30
RET_QK = RET_HEADS * RET_DK
RET_V = RET_HEADS * RET_DV
ML_W = MLSTM_HEADS * MLSTM_DH
N_GATES = 4 * MLSTM_HEADS
PROJ_SIZES = (RET_QK, RET_QK, RET_V, RET_V, ML_W, ML_W, ML_W, ML_W, N_GATES)
PROJ_COLS = sum(PROJ_SIZES)
SPLIT_AT = tuple(int(s) for s in np.cumsum(PROJ_SIZES)[:-1])


def _rmsnorm(x, g):
    xf = x.astype(jnp.float32)
    y = xf * lax.rsqrt(jnp.mean(xf * xf, axis=-1, keepdims=True) + EPS)
    return (y * g.astype(jnp.float32)).astype(x.dtype)

def _head_norm(y, g):
    mu = jnp.mean(y, axis=-1, keepdims=True)
    yc = y - mu
    var = jnp.mean(yc * yc, axis=-1, keepdims=True)
    out = (yc * lax.rsqrt(var + EPS)).reshape(y.shape[:2] + (-1,))
    return out * g.astype(jnp.float32)

def _rotary(x, pos):
    half = x.shape[-1] // 2
    inv = ROPE_BASE ** (-jnp.arange(half, dtype=jnp.float32) / half)
    ang = pos[:, None] * inv[None, :]
    cos = jnp.cos(ang)[None, :, None, :]
    sin = jnp.sin(ang)[None, :, None, :]
    x1, x2 = x[..., :half], x[..., half:]
    return jnp.concatenate([x1 * cos - x2 * sin, x2 * cos + x1 * sin], axis=-1)

def _pad_front(t, value=0.0):
    widths = [(0, 0)] * t.ndim
    widths[1] = (PAD_FRONT, 0)
    return jnp.pad(t, widths, constant_values=value)

def _flip(t):
    return jnp.flip(t, axis=1)

def _centred_conv(u, w, b):
    c = u.shape[-1]
    out = lax.conv_general_dilated(
        u, w.astype(u.dtype)[:, None, :], window_strides=(1,),
        padding=((CONV_K // 2, CONV_K // 2),),
        dimension_numbers=('NWC', 'WIO', 'NWC'), feature_group_count=c)
    return out + b.astype(u.dtype)

def _retention_dir(q, k, v, log_gamma):
    b_, t_, h_, dk = q.shape
    dv = v.shape[-1]
    nc = t_ // CHUNK
    q = q.reshape(b_, nc, CHUNK, h_, dk)
    k = k.reshape(b_, nc, CHUNK, h_, dk)
    v = v.reshape(b_, nc, CHUNK, h_, dv)
    idx = jnp.arange(CHUNK, dtype=jnp.float32)
    diff = idx[:, None] - idx[None, :]
    decay = jnp.where(diff >= 0, jnp.exp(log_gamma[:, None, None] * jnp.maximum(diff, 0.0)), 0.0)
    scores = jnp.einsum('bclhd,bcmhd->bchlm', q, k) * decay
    intra = jnp.einsum('bchlm,bcmhe->bclhe', scores, v)
    zeta = jnp.exp(log_gamma[:, None] * (CHUNK - 1.0 - idx)[None, :])
    upd = jnp.einsum('bclhd,bclhe,hl->bchde', k, v, zeta)
    g_chunk = jnp.exp(log_gamma * CHUNK)[:, None, None]

    def step(state, u_c):
        return g_chunk * state + u_c, state

    r0 = jnp.zeros((b_, h_, dk, dv), jnp.float32)
    _, r_prev = lax.scan(step, r0, jnp.moveaxis(upd, 1, 0))
    r_prev = jnp.moveaxis(r_prev, 0, 1)
    xi = jnp.exp(log_gamma[:, None] * (idx + 1.0)[None, :])
    cross = jnp.einsum('bclhd,bchde,hl->bclhe', q, r_prev, xi)
    return (intra + cross).reshape(b_, t_, h_, dv)

def _mlstm_dir(q, k, v, log_i, log_f):
    b_, t_, h_, d = q.shape
    nc = t_ // CHUNK
    q = q.reshape(b_, nc, CHUNK, h_, d)
    k = k.reshape(b_, nc, CHUNK, h_, d)
    v = v.reshape(b_, nc, CHUNK, h_, d)
    li = jnp.moveaxis(log_i.reshape(b_, nc, CHUNK, h_), 3, 2)
    lf = jnp.moveaxis(log_f.reshape(b_, nc, CHUNK, h_), 3, 2)
    bcum = jnp.cumsum(lf, axis=-1)
    b_last = bcum[..., -1]
    causal = jnp.tril(jnp.ones((CHUNK, CHUNK), dtype=bool))
    log_d = jnp.where(causal, bcum[..., :, None] - bcum[..., None, :] + li[..., None, :], NEG)
    log_u = b_last[..., None] - bcum + li
    a = jnp.max(log_u, axis=-1)
    w_u = jnp.exp(log_u - a[..., None])
    upd_c = jnp.einsum('bchl,bclhe,bclhd->bched', w_u, v, k)
    upd_n = jnp.einsum('bchl,bclhd->bchd', w_u, k)

    def step(carry, inp):
        c_st, n_st, m_st = carry
        uc, un, bl, ac = inp
        m_new = jnp.maximum(bl + m_st, ac)
        f = jnp.exp(bl + m_st - m_new)
        g = jnp.exp(ac - m_new)
        c_new = f[..., None, None] * c_st + g[..., None, None] * uc
        n_new = f[..., None] * n_st + g[..., None] * un
        return (c_new, n_new, m_new), (c_st, n_st, m_st)

    init = (jnp.zeros((b_, h_, d, d), jnp.float32),
            jnp.zeros((b_, h_, d), jnp.float32),
            jnp.zeros((b_, h_), jnp.float32))
    xs = (jnp.moveaxis(upd_c, 1, 0), jnp.moveaxis(upd_n, 1, 0),
          jnp.moveaxis(b_last, 1, 0), jnp.moveaxis(a, 1, 0))
    _, (c_prev, n_prev, m_prev) = lax.scan(step, init, xs)
    c_prev = jnp.moveaxis(c_prev, 0, 1)
    n_prev = jnp.moveaxis(n_prev, 0, 1)
    m_prev = jnp.moveaxis(m_prev, 0, 1)
    log_inter = bcum + m_prev[..., None]
    m_row = jnp.maximum(log_inter, jnp.max(log_d, axis=-1))
    s = jnp.einsum('bclhd,bcmhd->bchlm', q, k) * jnp.exp(log_d - m_row[..., None])
    w_inter = jnp.exp(log_inter - m_row)
    num = (jnp.einsum('bchlm,bcmhe->bclhe', s, v)
           + jnp.einsum('bclhd,bched,bchl->bclhe', q, c_prev, w_inter))
    den = jnp.sum(s, axis=-1) + jnp.einsum('bclhd,bchd,bchl->bchl', q, n_prev, w_inter)
    denom = jnp.maximum(jnp.abs(den), jnp.exp(-m_row))
    h = num / jnp.moveaxis(denom, 2, 3)[..., None]
    return h.reshape(b_, t_, h_, d)

def _token_mixer(h, norm_g, w_in, b_gates, conv_w, conv_b, ret_decay_logit,
                 ret_gn_g, mlstm_gn_g, w_out):
    b_, n_, _ = h.shape
    f32 = jnp.float32
    u = _rmsnorm(h, norm_g)
    proj = jnp.einsum('bnd,dk->bnk', u, w_in)
    rq, rk, rv, rg, mq, mk, mv, mo, gate_pre = jnp.split(proj, SPLIT_AT, axis=-1)

    pos = jnp.arange(n_, dtype=f32)
    rq = _rotary(rq.reshape(b_, n_, RET_HEADS, RET_DK).astype(f32), pos) * (RET_DK ** -0.5)
    rk = _rotary(rk.reshape(b_, n_, RET_HEADS, RET_DK).astype(f32), pos)
    rv = rv.reshape(b_, n_, RET_HEADS, RET_DV).astype(f32)
    rq, rk, rv = _pad_front(rq), _pad_front(rk), _pad_front(rv)
    log_gamma = jax.nn.log_sigmoid(ret_decay_logit.astype(f32))
    ret = (_retention_dir(rq, rk, rv, log_gamma[0])
           + _flip(_retention_dir(_flip(rq), _flip(rk), _flip(rv), log_gamma[1])))
    ret = ret[:, PAD_FRONT:]
    y_ret = _head_norm(ret, ret_gn_g) * jax.nn.silu(rg.astype(f32))

    qk = jax.nn.silu(_centred_conv(jnp.concatenate([mq, mk], axis=-1), conv_w, conv_b))
    mq, mk = jnp.split(qk, 2, axis=-1)
    mq = mq.reshape(b_, n_, MLSTM_HEADS, MLSTM_DH).astype(f32) * (MLSTM_DH ** -0.5)
    mk = mk.reshape(b_, n_, MLSTM_HEADS, MLSTM_DH).astype(f32)
    mv = mv.reshape(b_, n_, MLSTM_HEADS, MLSTM_DH).astype(f32)
    gts = gate_pre.astype(f32) + b_gates.astype(f32)
    log_i = gts[..., :2 * MLSTM_HEADS].reshape(b_, n_, 2, MLSTM_HEADS)
    log_f = jax.nn.log_sigmoid(gts[..., 2 * MLSTM_HEADS:]).reshape(b_, n_, 2, MLSTM_HEADS)
    mq, mk, mv = _pad_front(mq), _pad_front(mk), _pad_front(mv)
    log_i = _pad_front(log_i, NEG)
    log_f = _pad_front(log_f, 0.0)
    h_f = _mlstm_dir(mq, mk, mv, log_i[:, :, 0], log_f[:, :, 0])
    h_b = _flip(_mlstm_dir(_flip(mq), _flip(mk), _flip(mv),
                           _flip(log_i[:, :, 1]), _flip(log_f[:, :, 1])))
    hm = (h_f + h_b)[:, PAD_FRONT:]
    hm = jax.nn.sigmoid(mo.astype(f32)).reshape(b_, n_, MLSTM_HEADS, MLSTM_DH) * hm
    y_m = _head_norm(hm, mlstm_gn_g)

    y = jnp.concatenate([y_ret, y_m], axis=-1).astype(h.dtype)
    return jnp.einsum('bnk,kd->bnd', y, w_out)

def _expert_choice_ffn(h, norm_g, w_router, w_gate, w_up, w_down):
    b_, n_, _ = h.shape
    u = _rmsnorm(h, norm_g)
    aff = jax.nn.softmax(jnp.einsum('bnd,de->bne', u, w_router).astype(jnp.float32), axis=-1)
    cap = EC_CAPACITY * n_ // N_EXPERTS
    g, idx = lax.top_k(jnp.swapaxes(aff, 1, 2), cap)
    xs = jax.vmap(lambda ub, ib: ub[ib])(u, idx)
    hid = (jax.nn.silu(jnp.einsum('becd,edf->becf', xs, w_gate))
           * jnp.einsum('becd,edf->becf', xs, w_up))
    y = jnp.einsum('becf,efd->becd', hid, w_down) * g[..., None].astype(h.dtype)
    return jnp.zeros_like(h).at[jnp.arange(b_)[:, None, None], idx].add(y)

def first_inputs(seed: int = 0) -> dict:
    key = jax.random.key(seed)
    ks = jax.random.split(key, 17)
    f32 = jnp.float32
    nrm = jax.random.normal
    x = nrm(ks[0], (BATCH, SEQ, D_MODEL), f32)
    meta_tokens = nrm(ks[1], (N_META, D_MODEL), f32)
    mix_norm_g = 1.0 + 0.05 * nrm(ks[2], (DEPTH, D_MODEL), f32)
    w_in = nrm(ks[3], (DEPTH, D_MODEL, PROJ_COLS), f32) * (D_MODEL ** -0.5)
    f_bias = jnp.tile(jnp.linspace(3.0, 6.0, MLSTM_HEADS, dtype=f32), 2)
    base_gates = jnp.concatenate([jnp.zeros((2 * MLSTM_HEADS,), f32), f_bias])
    b_gates = base_gates[None, :] + 0.1 * nrm(ks[4], (DEPTH, N_GATES), f32)
    conv_w = nrm(ks[5], (DEPTH, CONV_K, 2 * ML_W), f32) * (CONV_K ** -0.5)
    conv_b = 0.01 * nrm(ks[6], (DEPTH, 2 * ML_W), f32)
    scales = 5.0 + jnp.arange(RET_HEADS, dtype=f32)
    gamma_logit = jnp.log(2.0 ** scales - 1.0)
    ret_decay_logit = gamma_logit[None, None, :] + 0.05 * nrm(ks[7], (DEPTH, 2, RET_HEADS), f32)
    ret_gn_g = 1.0 + 0.05 * nrm(ks[8], (DEPTH, RET_V), f32)
    mlstm_gn_g = 1.0 + 0.05 * nrm(ks[9], (DEPTH, ML_W), f32)
    w_out = nrm(ks[10], (DEPTH, D_MIX, D_MODEL), f32) * (D_MIX ** -0.5)
    ffn_norm_g = 1.0 + 0.05 * nrm(ks[11], (DEPTH, D_MODEL), f32)
    w_router = nrm(ks[12], (DEPTH, D_MODEL, N_EXPERTS), f32) * (D_MODEL ** -0.5)
    w_gate = nrm(ks[13], (DEPTH, N_EXPERTS, D_MODEL, D_FF), f32) * (D_MODEL ** -0.5)
    w_up = nrm(ks[14], (DEPTH, N_EXPERTS, D_MODEL, D_FF), f32) * (D_MODEL ** -0.5)
    w_down = nrm(ks[15], (DEPTH, N_EXPERTS, D_FF, D_MODEL), f32) * (D_FF ** -0.5)
    final_norm_g = 1.0 + 0.05 * nrm(ks[16], (D_MODEL,), f32)
    return {'x': x, 'meta_tokens': meta_tokens, 'mix_norm_g': mix_norm_g, 'w_in': w_in,
            'b_gates': b_gates, 'conv_w': conv_w, 'conv_b': conv_b,
            'ret_decay_logit': ret_decay_logit, 'ret_gn_g': ret_gn_g, 'mlstm_gn_g': mlstm_gn_g,
            'w_out': w_out, 'ffn_norm_g': ffn_norm_g, 'w_router': w_router, 'w_gate': w_gate,
            'w_up': w_up, 'w_down': w_down, 'final_norm_g': final_norm_g}

def first_block(x, meta_tokens, mix_norm_g, w_in, b_gates, conv_w, conv_b, ret_decay_logit,
              ret_gn_g, mlstm_gn_g, w_out, ffn_norm_g, w_router, w_gate, w_up, w_down,
              final_norm_g):
    b_ = x.shape[0]
    meta = jnp.broadcast_to(meta_tokens.astype(x.dtype)[None], (b_, N_META, x.shape[-1]))
    h = jnp.concatenate([meta, x], axis=1)
    for l in range(DEPTH):
        h = h + _token_mixer(h, mix_norm_g[l], w_in[l], b_gates[l], conv_w[l], conv_b[l],
                             ret_decay_logit[l], ret_gn_g[l], mlstm_gn_g[l], w_out[l])
        h = h + _expert_choice_ffn(h, ffn_norm_g[l], w_router[l], w_gate[l], w_up[l], w_down[l])
    h = _rmsnorm(h, final_norm_g)
    return h[:, N_META:]


CTX_LEN = 256
GRID_W = 64
H_A = 4
DK_A = 128
DV_A = 128
C_A = H_A * DV_A
SHORT_CONV = 5
CHUNK_2 = 64
H_B = 8
N_B = 64
C_B = H_B * N_B
LORA_W = 64
LORA_A = 64
LORA_G = 128
A_COLS = 4 * C_A + 4 * H_A
B_COLS = 3 * C_B + 2 * LORA_W + 2 * LORA_A + LORA_G
IN_COLS = A_COLS + B_COLS + 2 * D_MODEL
N_GROUPS = 4
EXPERTS_PER_GROUP = 8
N_EXPERTS_2 = N_GROUPS * EXPERTS_PER_GROUP
TOP_K = 2
D_EXPERT = 256
NORM_EPS = 1e-6
LNX_EPS = 1e-5 * N_B


def rmsnorm(x, g):
    xf = x.astype(jnp.float32)
    y = xf * lax.rsqrt(jnp.mean(xf * xf, axis=-1, keepdims=True) + NORM_EPS)
    return y.astype(x.dtype) * g

def l2norm(x):
    xf = x.astype(jnp.float32)
    return (xf * lax.rsqrt(jnp.sum(xf * xf, axis=-1, keepdims=True) + NORM_EPS)).astype(x.dtype)

def modulate(x, shift, scale):
    return x * (1 + scale) + shift

def both_dirs(t):
    return jnp.stack([t, jnp.flip(t, 1)], 0)

def per_dir(t):
    return jnp.stack([t[:, :, 0], jnp.flip(t[:, :, 1], 1)], 0)

def merge_dirs(y):
    return y[0] + jnp.flip(y[1], 1)

def to_col_major(x, rows):
    b, l, c = x.shape
    return x.reshape(b, rows, GRID_W, c).transpose(0, 2, 1, 3).reshape(b, l, c)

def to_row_major(x, rows):
    b, l, c = x.shape
    return x.reshape(b, GRID_W, rows, c).transpose(0, 2, 1, 3).reshape(b, l, c)

def depthwise_conv(x, w):
    pad = SHORT_CONV // 2
    return lax.conv_general_dilated(x, w[:, None, :], window_strides=(1,), padding=[(pad, pad)],
                                    dimension_numbers=('NWC', 'WIO', 'NWC'),
                                    feature_group_count=x.shape[-1])

def bidir_shift(x):
    xp = jnp.pad(x, ((0, 0), (1, 1), (0, 0)))
    return 0.5 * (xp[:, :-2] + xp[:, 2:])

def gated_delta_chunked(q, k, v, g, beta, s0):
    dtype = v.dtype
    q, k, v, g, beta = (t.astype(jnp.float32) for t in (q, k, v, g, beta))
    n = q.shape[-2] // CHUNK_2
    dv = v.shape[-1]

    def blk(t):
        return t.reshape(t.shape[:-2] + (n, CHUNK_2, t.shape[-1]))

    q, k, v = blk(q), blk(k), blk(v)
    g = g.reshape(g.shape[:-1] + (n, CHUNK_2))
    beta = beta.reshape(beta.shape[:-1] + (n, CHUNK_2))
    gc = jnp.cumsum(g, axis=-1)
    incl = jnp.tril(jnp.ones((CHUNK_2, CHUNK_2), bool))
    strict = jnp.tril(jnp.ones((CHUNK_2, CHUNK_2), bool), -1)
    decay = jnp.where(incl, jnp.exp(jnp.where(incl, gc[..., :, None] - gc[..., None, :], 0.0)), 0.0)
    k_beta = k * beta[..., None]
    lower = jnp.where(strict, jnp.einsum('...id,...jd->...ij', k_beta, k) * decay, 0.0)
    a_mat = jnp.eye(CHUNK_2, dtype=jnp.float32) + lower
    rhs = jnp.concatenate([v * beta[..., None], k_beta * jnp.exp(gc)[..., None]], axis=-1)
    sol = lax.linalg.triangular_solve(a_mat, rhs, left_side=True, lower=True, unit_diagonal=True)
    u, w = sol[..., :dv], sol[..., dv:]
    qk = jnp.where(incl, jnp.einsum('...id,...jd->...ij', q, k) * decay, 0.0)
    q_dec = q * jnp.exp(gc)[..., None]
    k_dec = k * jnp.exp(gc[..., -1:] - gc)[..., None]
    g_end = jnp.exp(gc[..., -1])
    xs = (jnp.moveaxis(u, -3, 0), jnp.moveaxis(w, -3, 0), jnp.moveaxis(qk, -3, 0),
          jnp.moveaxis(q_dec, -3, 0), jnp.moveaxis(k_dec, -3, 0), jnp.moveaxis(g_end, -1, 0))

    def step(s, inp):
        u_c, w_c, qk_c, qd_c, kd_c, ge_c = inp
        v_new = u_c - jnp.einsum('...ck,...kv->...cv', w_c, s)
        o_c = jnp.einsum('...ck,...kv->...cv', qd_c, s) + jnp.einsum('...ij,...jv->...iv', qk_c, v_new)
        s = s * ge_c[..., None, None] + jnp.einsum('...ck,...cv->...kv', kd_c, v_new)
        return s, o_c

    s_fin, o = lax.scan(step, s0.astype(jnp.float32), xs)
    o = jnp.moveaxis(o, 0, -3)
    return o.reshape(o.shape[:-3] + (n * CHUNK_2, dv)).astype(dtype), s_fin

def gdn_branch(cols, s0, conv_w, a_log, dt_bias, onorm_g):
    bsz, length, _ = cols.shape
    qkv, z, a, bt = jnp.split(cols, [3 * C_A, 4 * C_A, 4 * C_A + 2 * H_A], axis=-1)
    qkv = jax.nn.silu(depthwise_conv(qkv, conv_w))
    q, k, v = (t.reshape(bsz, length, H_A, DK_A) for t in jnp.split(qkv, 3, axis=-1))
    q = l2norm(q) * DK_A ** -0.5
    k = l2norm(k)
    g = -jnp.exp(a_log) * jax.nn.softplus(a.reshape(bsz, length, 2, H_A) + dt_bias)
    beta = jax.nn.sigmoid(bt.reshape(bsz, length, 2, H_A))
    sw = lambda t: jnp.swapaxes(t, 2, 3)
    o, s_fin = gated_delta_chunked(sw(both_dirs(q)), sw(both_dirs(k)), sw(both_dirs(v)),
                                   sw(per_dir(g)), sw(per_dir(beta)), s0)
    o = merge_dirs(sw(o))
    o = rmsnorm(o, onorm_g) * jax.nn.silu(z.reshape(bsz, length, H_A, DV_A))
    return o.reshape(bsz, length, C_A), s_fin

def rwkv7_scan(r, w, k, v, a, b, s0):
    dtype = r.dtype
    xs = tuple(jnp.moveaxis(t.astype(jnp.float32), 2, 0) for t in (r, w, k, v, a, b))

    def step(s, inp):
        r_t, w_t, k_t, v_t, a_t, b_t = inp
        sa = jnp.einsum('...vk,...k->...v', s, a_t)
        s = s * w_t[..., None, :] + sa[..., :, None] * b_t[..., None, :] + v_t[..., :, None] * k_t[..., None, :]
        return s, jnp.einsum('...vk,...k->...v', s, r_t)

    s_fin, y = lax.scan(step, s0.astype(jnp.float32), xs)
    return jnp.moveaxis(y, 0, 2).astype(dtype), s_fin

def rwkv_branch(cols, s0, mu, w0, w2, a0, a2, g2, k_k, k_a, r_k, lnx_g, lnx_b):
    bsz, length, _ = cols.shape
    cols = cols + (bidir_shift(cols) - cols) * mu
    r, k, v, w_lo, a_lo, g_lo = jnp.split(
        cols, [C_B, 2 * C_B, 3 * C_B, 3 * C_B + 2 * LORA_W, 3 * C_B + 2 * LORA_W + 2 * LORA_A], axis=-1)
    w_lo = w_lo.reshape(bsz, length, 2, LORA_W)
    a_lo = a_lo.reshape(bsz, length, 2, LORA_A)
    w_log = -jax.nn.softplus(-(w0 + jnp.einsum('bldr,drc->bldc', jnp.tanh(w_lo), w2))) - 0.5
    decay = jnp.exp(-jnp.exp(w_log.astype(jnp.float32))).astype(cols.dtype)
    iclr = jax.nn.sigmoid(a0 + jnp.einsum('bldr,drc->bldc', a_lo, a2))
    gate = jax.nn.sigmoid(g_lo) @ g2
    heads = lambda t: t.reshape(t.shape[:-1] + (H_B, N_B))
    kk = l2norm(heads(k * k_k))
    k_dir = heads(k[:, :, None, :] * (1 + (iclr - 1) * k_a))
    b_dir = kk[:, :, None] * heads(iclr)
    r_h, v_h = heads(r), heads(v)
    y, s_fin = rwkv7_scan(both_dirs(r_h), per_dir(heads(decay)), per_dir(k_dir), both_dirs(v_h),
                          both_dirs(-kk), per_dir(b_dir), s0)
    yf = merge_dirs(y).astype(jnp.float32)
    mean = jnp.mean(yf, axis=-1, keepdims=True)
    var = jnp.mean(jnp.square(yf - mean), axis=-1, keepdims=True)
    y = ((yf - mean) * lax.rsqrt(var + LNX_EPS)).astype(cols.dtype).reshape(bsz, length, C_B) * lnx_g + lnx_b
    bonus = jnp.einsum('blhn,bldhn,hn->blh', r_h, k_dir, r_k)[..., None] * v_h
    y = (y + bonus.reshape(bsz, length, C_B)) * gate
    return y, s_fin

def merge_branches(gates, o_a, o_b, w_o_a, w_o_b, w_out):
    g_a, g_b = jnp.split(gates, 2, axis=-1)
    y = jax.nn.sigmoid(g_a) * (o_a @ w_o_a) + jax.nn.sigmoid(g_b) * (o_b @ w_o_b)
    return y @ w_out

def mixing_sublayer(u_lat, u_ctx, rows, with_ctx_out, w_in, gdn_conv, gdn_a_log, gdn_dt_bias, gdn_onorm_g,
                    rwkv_mu, rwkv_w0, rwkv_w2, rwkv_a0, rwkv_a2, rwkv_g2, rwkv_k_k, rwkv_k_a, rwkv_r_k,
                    rwkv_lnx_g, rwkv_lnx_b, w_o_a, w_o_b, w_out):
    bsz = u_lat.shape[0]
    split_at = [A_COLS, A_COLS + B_COLS]
    a_lat, b_lat, gates_lat = jnp.split(u_lat @ w_in, split_at, axis=-1)
    a_ctx, b_ctx, gates_ctx = jnp.split(u_ctx @ w_in, split_at, axis=-1)

    def run_a(cols, s0):
        return gdn_branch(cols, s0, gdn_conv, gdn_a_log, gdn_dt_bias, gdn_onorm_g)

    def run_b(cols, s0):
        return rwkv_branch(cols, s0, rwkv_mu, rwkv_w0, rwkv_w2, rwkv_a0, rwkv_a2, rwkv_g2,
                           rwkv_k_k, rwkv_k_a, rwkv_r_k, rwkv_lnx_g, rwkv_lnx_b)

    zeros_a = jnp.zeros((2, bsz, H_A, DK_A, DV_A), jnp.float32)
    zeros_b = jnp.zeros((2, bsz, H_B, N_B, N_B), jnp.float32)
    oa_ctx, state_a = run_a(a_ctx, zeros_a)
    ob_ctx, state_b = run_b(b_ctx, zeros_b)
    oa_lat, _ = run_a(a_lat, state_a)
    ob_lat, _ = run_b(to_col_major(b_lat, rows), state_b)
    ob_lat = to_row_major(ob_lat, rows)
    y_lat = merge_branches(gates_lat, oa_lat, ob_lat, w_o_a, w_o_b, w_out)
    if not with_ctx_out:
        return y_lat, None
    return y_lat, merge_branches(gates_ctx, oa_ctx, ob_ctx, w_o_a, w_o_b, w_out)

def hier_moe(h, router_grp, router_grp_b, router_exp, router_exp_b, w_gate, w_up, w_down):
    shape = h.shape
    t = h.reshape(-1, shape[-1])
    grp_p = jax.nn.softmax((t @ router_grp + router_grp_b).astype(jnp.float32), axis=-1)
    p_grp, g_sel = lax.top_k(grp_p, 1)
    exp_logits = (t @ router_exp + router_exp_b).astype(jnp.float32).reshape(-1, N_GROUPS, EXPERTS_PER_GROUP)
    in_grp = jnp.take_along_axis(exp_logits, g_sel[:, :, None], axis=1)[:, 0]
    top_logit, top_idx = lax.top_k(in_grp, TOP_K)
    w_top = jax.nn.softmax(top_logit, axis=-1) * p_grp
    w_exp = jnp.einsum('tk,tke->te', w_top, jax.nn.one_hot(top_idx, EXPERTS_PER_GROUP, dtype=jnp.float32))
    combine = (jax.nn.one_hot(g_sel[:, 0], N_GROUPS, dtype=jnp.float32)[:, :, None]
               * w_exp[:, None, :]).astype(h.dtype)
    out = jnp.zeros_like(t)
    for grp in range(N_GROUPS):
        hid = jax.nn.silu(jnp.einsum('td,edf->tef', t, w_gate[grp])) * jnp.einsum('td,edf->tef', t, w_up[grp])
        out = out + jnp.einsum('tef,efd->td', hid * combine[:, grp, :, None], w_down[grp])
    return out.reshape(shape)

def second_inputs(seed: int = 0) -> dict:
    key = jax.random.key(seed)
    ks = jax.random.split(key, 36)
    d = D_MODEL
    nl = DEPTH

    def nrm(k, shape, scale):
        return jax.random.normal(k, shape, jnp.float32) * scale

    dt = jnp.exp(jax.random.uniform(ks[11], (nl, 2, H_A), minval=math.log(1e-3), maxval=math.log(1e-1)))
    return {
        'x': nrm(ks[0], (BATCH, SEQ, d), 1.0),
        'c': nrm(ks[1], (BATCH, d), 1.0),
        'ctx': nrm(ks[2], (BATCH, CTX_LEN, d), 1.0),
        'c_ctx': nrm(ks[3], (d,), 1.0),
        'ada_w': nrm(ks[4], (nl, d, 6 * d), 0.5 * d ** -0.5),
        'ada_b': nrm(ks[5], (nl, 6 * d), 0.01),
        'norm_mix_g': 1.0 + nrm(ks[6], (nl, d), 0.05),
        'norm_ffn_g': 1.0 + nrm(ks[7], (nl, d), 0.05),
        'w_in': nrm(ks[8], (nl, d, IN_COLS), d ** -0.5),
        'gdn_conv': nrm(ks[9], (nl, SHORT_CONV, 3 * C_A), SHORT_CONV ** -0.5),
        'gdn_a_log': jnp.log(jax.random.uniform(ks[10], (nl, 2, H_A), minval=1.0, maxval=16.0)),
        'gdn_dt_bias': dt + jnp.log(-jnp.expm1(-dt)),
        'gdn_onorm_g': 1.0 + nrm(ks[12], (nl, DV_A), 0.05),
        'rwkv_mu': jax.random.uniform(ks[13], (nl, B_COLS)),
        'rwkv_w0': jax.random.uniform(ks[14], (nl, 2, C_B), minval=-6.0, maxval=-1.0),
        'rwkv_w2': nrm(ks[15], (nl, 2, LORA_W, C_B), 0.1),
        'rwkv_a0': nrm(ks[16], (nl, 2, C_B), 0.1),
        'rwkv_a2': nrm(ks[17], (nl, 2, LORA_A, C_B), 0.1),
        'rwkv_g2': nrm(ks[18], (nl, LORA_G, C_B), LORA_G ** -0.5),
        'rwkv_k_k': 0.85 + nrm(ks[19], (nl, C_B), 0.05),
        'rwkv_k_a': 1.0 + nrm(ks[20], (nl, C_B), 0.05),
        'rwkv_r_k': nrm(ks[21], (nl, H_B, N_B), 0.1),
        'rwkv_lnx_g': 1.0 + nrm(ks[22], (nl, C_B), 0.05),
        'rwkv_lnx_b': nrm(ks[23], (nl, C_B), 0.01),
        'w_o_a': nrm(ks[24], (nl, C_A, d), C_A ** -0.5),
        'w_o_b': nrm(ks[25], (nl, C_B, d), C_B ** -0.5),
        'w_out': nrm(ks[26], (nl, d, d), d ** -0.5),
        'router_grp': nrm(ks[27], (nl, d, N_GROUPS), d ** -0.5),
        'router_grp_b': nrm(ks[28], (nl, N_GROUPS), 0.01),
        'router_exp': nrm(ks[29], (nl, d, N_EXPERTS_2), d ** -0.5),
        'router_exp_b': nrm(ks[30], (nl, N_EXPERTS_2), 0.01),
        'moe_w_gate': nrm(ks[31], (nl, N_GROUPS, EXPERTS_PER_GROUP, d, D_EXPERT), d ** -0.5),
        'moe_w_up': nrm(ks[32], (nl, N_GROUPS, EXPERTS_PER_GROUP, d, D_EXPERT), d ** -0.5),
        'moe_w_down': nrm(ks[33], (nl, N_GROUPS, EXPERTS_PER_GROUP, D_EXPERT, d), D_EXPERT ** -0.5),
        'final_norm_g': 1.0 + nrm(ks[34], (d,), 0.05),
    }

def second_block(x, c, ctx, c_ctx, ada_w, ada_b, norm_mix_g, norm_ffn_g, w_in, gdn_conv, gdn_a_log, gdn_dt_bias,
              gdn_onorm_g, rwkv_mu, rwkv_w0, rwkv_w2, rwkv_a0, rwkv_a2, rwkv_g2, rwkv_k_k, rwkv_k_a, rwkv_r_k,
              rwkv_lnx_g, rwkv_lnx_b, w_o_a, w_o_b, w_out, router_grp, router_grp_b, router_exp, router_exp_b,
              moe_w_gate, moe_w_up, moe_w_down, final_norm_g):
    rows = x.shape[1] // GRID_W
    s_lat = jax.nn.silu(c)[:, None, :]
    s_ctx = jax.nn.silu(c_ctx)
    h_lat, h_ctx = x, ctx
    for l in range(DEPTH):
        last = l == DEPTH - 1
        m_lat = jnp.split(s_lat @ ada_w[l] + ada_b[l], 6, axis=-1)
        m_ctx = jnp.split(s_ctx @ ada_w[l] + ada_b[l], 6, axis=-1)
        u_lat = modulate(rmsnorm(h_lat, norm_mix_g[l]), m_lat[0], m_lat[1])
        u_ctx = modulate(rmsnorm(h_ctx, norm_mix_g[l]), m_ctx[0], m_ctx[1])
        y_lat, y_ctx = mixing_sublayer(
            u_lat, u_ctx, rows, not last, w_in[l], gdn_conv[l], gdn_a_log[l], gdn_dt_bias[l], gdn_onorm_g[l],
            rwkv_mu[l], rwkv_w0[l], rwkv_w2[l], rwkv_a0[l], rwkv_a2[l], rwkv_g2[l], rwkv_k_k[l], rwkv_k_a[l],
            rwkv_r_k[l], rwkv_lnx_g[l], rwkv_lnx_b[l], w_o_a[l], w_o_b[l], w_out[l])
        h_lat = h_lat + m_lat[2] * y_lat
        h_lat = h_lat + m_lat[5] * hier_moe(
            modulate(rmsnorm(h_lat, norm_ffn_g[l]), m_lat[3], m_lat[4]), router_grp[l], router_grp_b[l],
            router_exp[l], router_exp_b[l], moe_w_gate[l], moe_w_up[l], moe_w_down[l])
        if not last:
            h_ctx = h_ctx + m_ctx[2] * y_ctx
            h_ctx = h_ctx + m_ctx[5] * hier_moe(
                modulate(rmsnorm(h_ctx, norm_ffn_g[l]), m_ctx[3], m_ctx[4]), router_grp[l], router_grp_b[l],
                router_exp[l], router_exp_b[l], moe_w_gate[l], moe_w_up[l], moe_w_down[l])
    return rmsnorm(h_lat, final_norm_g)


def setup_inputs(seed=0):
    out = dict(first_inputs(seed))
    for name, value in second_inputs(seed + 1).items():
        if name != "x":
            out[name + "_2"] = value
    return out


def reference(
    x, meta_tokens, mix_norm_g, w_in, b_gates, conv_w, conv_b, ret_decay_logit, ret_gn_g,
    mlstm_gn_g, w_out, ffn_norm_g, w_router, w_gate, w_up, w_down, final_norm_g, c_2, ctx_2,
    c_ctx_2, ada_w_2, ada_b_2, norm_mix_g_2, norm_ffn_g_2, w_in_2, gdn_conv_2, gdn_a_log_2,
    gdn_dt_bias_2, gdn_onorm_g_2, rwkv_mu_2, rwkv_w0_2, rwkv_w2_2, rwkv_a0_2, rwkv_a2_2,
    rwkv_g2_2, rwkv_k_k_2, rwkv_k_a_2, rwkv_r_k_2, rwkv_lnx_g_2, rwkv_lnx_b_2, w_o_a_2, w_o_b_2,
    w_out_2, router_grp_2, router_grp_b_2, router_exp_2, router_exp_b_2, moe_w_gate_2,
    moe_w_up_2, moe_w_down_2, final_norm_g_2,
):
    x = first_block(
        x, meta_tokens, mix_norm_g, w_in, b_gates, conv_w, conv_b, ret_decay_logit, ret_gn_g,
        mlstm_gn_g, w_out, ffn_norm_g, w_router, w_gate, w_up, w_down, final_norm_g,
    )
    return second_block(
        x, c_2, ctx_2, c_ctx_2, ada_w_2, ada_b_2, norm_mix_g_2, norm_ffn_g_2, w_in_2,
        gdn_conv_2, gdn_a_log_2, gdn_dt_bias_2, gdn_onorm_g_2, rwkv_mu_2, rwkv_w0_2, rwkv_w2_2,
        rwkv_a0_2, rwkv_a2_2, rwkv_g2_2, rwkv_k_k_2, rwkv_k_a_2, rwkv_r_k_2, rwkv_lnx_g_2,
        rwkv_lnx_b_2, w_o_a_2, w_o_b_2, w_out_2, router_grp_2, router_grp_b_2, router_exp_2,
        router_exp_b_2, moe_w_gate_2, moe_w_up_2, moe_w_down_2, final_norm_g_2,
    )


_drawn_inputs = setup_inputs


def setup_inputs(seed=0):
    import zlib

    import numpy as np

    out = dict(_drawn_inputs(seed))
    spreads = {}
    factors = {'conv_b': 4.911,
     'ada_b_2': 4.355,
     'norm_mix_g_2': 3.356,
     'norm_ffn_g_2': 2.678,
     'gdn_a_log_2': 3.359,
     'gdn_onorm_g_2': 6.382,
     'rwkv_w2_2': 5.988,
     'rwkv_a0_2': 5.411,
     'rwkv_k_k_2': 16.72,
     'rwkv_k_a_2': 3.621,
     'rwkv_lnx_g_2': 27.5,
     'rwkv_lnx_b_2': 180.083,
     'router_grp_b_2': 196.084,
     'router_exp_b_2': 22.429,
     'c_ctx_2': 2.819}
    for name, (base, spread) in spreads.items():
        noise = np.random.default_rng([zlib.crc32(name.encode()), seed]).standard_normal(out[name].shape)
        drawn = base * np.exp(spread * noise) if base else spread * noise
        out[name] = jnp.asarray(drawn.astype(out[name].dtype))
    for name, factor in factors.items():
        out[name] = (out[name] * factor).astype(out[name].dtype)
    return out
```

```python
from contextlib import ExitStack, contextmanager

import concourse.bass as bass
from concourse import mybir
import numpy as np

F32 = mybir.dt.float32
ALU = mybir.AluOpType
ACT = mybir.ActivationFunctionType
AX_X = mybir.AxisListType.X

P = 128
BANK = 512
D = 1024
KT = D // P
SEQ, N_META = 256, 16
TOKS = N_META + SEQ
TILES = [(N_META, 0), (P, N_META), (P, N_META + P)]
TILES2 = [(P, 0), (P, P)]
H1 = 4
EPS = 1e-6
N_EXP, CAP = 16, 2 * TOKS // 16
SLOT = 64
PAIRS = N_EXP // 2
FF = 2816
FT = FF // P
RING, PIECE = 6, FF

PARAMS = [
    [("mix_norm_g", 8), ("conv_w", 40), ("conv_b", 8), ("ret_gn_g", 4), ("mlstm_gn_g", 4), ("ffn_norm_g", 8),
     ("norm_mix_g_2", 8), ("norm_ffn_g_2", 8), ("gdn_onorm_g_2", 1), ("rwkv_mu_2", 15)],
    [("ada_b_2", 48), ("gdn_conv_2", 60)],
    [("c_2", 8), ("c_ctx_2", 8), ("rwkv_w0_2", 8), ("rwkv_a0_2", 8), ("rwkv_k_k_2", 4), ("rwkv_k_a_2", 4),
     ("rwkv_r_k_2", 4), ("rwkv_lnx_g_2", 4), ("rwkv_lnx_b_2", 4)],
]

def param_columns():
    at, col = {}, 0
    for batch in PARAMS:
        for name, rows in batch:
            at[name] = col
            col += rows
    return at, col

CONSTS = [("ident", P), ("ones", P), ("half_ones", P), ("tri_le", P), ("tri_ge", P), ("tri_lt", P), ("tri_gt", P),
          ("iota", SLOT)]
CONSTS_A = [("rot", P), ("cos", TOKS), ("sin", TOKS), ("cosq", TOKS), ("sinq", TOKS), ("pos", TOKS), ("posj", 3)]
CONSTS_B = [("join", 14 * P)]

def constant_arrays():
    i = np.arange(P)
    row, colm = i[:, None], i[None, :]
    c = {
        "ident": np.eye(P), "ones": np.ones((P, P)), "half_ones": (row // 64 == colm // 64) * 1.0,
        "tri_le": (row <= colm) * 1.0, "tri_ge": (row >= colm) * 1.0,
        "tri_lt": (row < colm) * 1.0, "tri_gt": (row > colm) * 1.0,
        "iota": np.broadcast_to(np.arange(SLOT), (P, SLOT)),
    }
    half = P // 2
    c["rot"] = (row == colm - half) * 1.0 - (row == colm + half) * 1.0
    inv = (np.float32(10000.0) ** (-(np.arange(half, dtype=np.float32)) / np.float32(half))).astype(np.float32)
    ang = (np.arange(TOKS, dtype=np.float32)[None, :] * inv[:, None]).astype(np.float32)
    cos, sin = (np.concatenate([f(ang), f(ang)]) for f in (np.cos, np.sin))
    c |= {"cos": cos, "sin": sin, "cosq": cos * P ** -0.5, "sinq": sin * P ** -0.5,
          "pos": np.broadcast_to(np.arange(TOKS), (P, TOKS)),
          "posj": np.stack([i + off for _, off in TILES], 1)}
    lower = [((row // s) % 2 == 1) & ((colm // s) == (row // s) - 1) for s in (1, 2, 4, 8, 16, 32, 64)]
    c["join"] = np.concatenate([*lower, *(m.T for m in lower)], 1) * 1.0
    return [np.concatenate([c[n] for n, _ in group], 1).astype(np.float32) for group in (CONSTS, CONSTS_A, CONSTS_B)]

def build(nc, A, consts, out, debug=None):
    given, taken = {}, {}
    DBG = debug

    with ExitStack() as ctx:
        def sem(name):
            s = ctx.enter_context(nc.semaphore(name))
            given[name] = 0
            return s

        loops = {}

        def passed(eng, s):
            if str(eng.engine) not in loops:
                return 0
            i, per = loops[str(eng.engine)]
            return i * per[s.name]

        def up(s, n=1):
            given[s.name] += n
            return n

        def due(eng, s, n=1):
            key = (str(eng.engine), s.name)
            taken[key] = taken.get(key, 0) + n
            return passed(eng, s) + taken[key]

        def own(eng, s):
            return passed(eng, s) + given[s.name]

        @contextmanager
        def looped(eng, n, per):
            g0, t0 = dict(given), dict(taken)
            with eng.Fori(0, n) as i:
                loops[str(eng.engine)] = (i, per)
                yield i
                del loops[str(eng.engine)]
            for name in given:
                if given[name] != g0[name]:
                    assert given[name] - g0[name] == per[name], (name, given[name] - g0[name], per[name])
                    given[name] += (n - 1) * per[name]
            for key in taken:
                if key[0] == str(eng.engine) and taken[key] != t0.get(key, 0):
                    assert taken[key] - t0.get(key, 0) == per[key[1]], (key, taken[key] - t0.get(key, 0))
                    taken[key] += (n - 1) * per[key[1]]

        def sb(name, cols):
            return ctx.enter_context(nc.sbuf_tensor(name, [P, cols], F32))

        ps = [ctx.enter_context(nc.psum_tensor(f"bank{i}", [P, BANK], F32)) for i in range(8)]
        ring = sb("ring", RING * PIECE)
        landed = [sem(f"slot{i}_landed") for i in range(RING)]
        piece_used = sem("piece_used")
        inputs_landed = sem("inputs_landed")
        phase_ended = sem("phase_ended")
        dve_order, act_order, pool_order = sem("dve_order"), sem("act_order"), sem("pool_order")
        out_written = sem("out_written")

        phases = {}

        def phase_end(eng):
            phases[str(eng.engine)] = phases.get(str(eng.engine), 0) + 1
            return 4 * phases[str(eng.engine)]

        pieces = []
        slot_count = [0] * RING

        def piece(src, floats, shape, names):
            n = len(pieces)
            k = n % RING
            slot_count[k] += 1
            view = ring[:, k * PIECE:k * PIECE + floats].rearrange(shape, **names)
            pieces.append((src, view, k, 16 * slot_count[k]))
            return view, landed[k], 16 * slot_count[k], n

        def after(views):
            return views[-1][3] + 1

        def column_pieces(w, c0, cols, halves=2):
            kts = KT // halves
            return [piece(w[h * kts * P:(h + 1) * kts * P, c0:c0 + cols].rearrange("(k p) c -> p k c", p=P),
                          kts * cols, "p (k c) -> p k c", {"k": kts}) for h in range(halves)]

        def rows_pieces(w, rows_at_once=2):
            n = w.shape[0] // P
            return [piece(w[i * P:min(i + rows_at_once, n) * P, :].rearrange("(k p) c -> p k c", p=P),
                          min(rows_at_once, n - i) * D, "p (k c) -> p k c", {"k": min(rows_at_once, n - i)})
                    for i in range(0, n, rows_at_once)]

        GC = sum(n for _, n in CONSTS)
        cst_all = sb("consts", GC)
        C = {}
        at = 0
        for name, n in CONSTS:
            C[name] = cst_all[:, at:at + n]
            at += n
        PCOL, n_params = param_columns()
        prm = sb("params", n_params)
        arena = sb("arena", 53215 - RING * PIECE - GC - n_params - 64)
        small = sb("small", 48)
        eps_col = small[:, 0:1]
        top = [0]

        def ar(cols, shape=None, **names):
            v = arena[:, top[0]:top[0] + cols]
            top[0] += cols
            assert top[0] <= arena.shape[1], top[0]
            return v.rearrange(shape, **names) if shape else v

        def pc(name, i):
            return prm[:, PCOL[name] + i:PCOL[name] + i + 1]

        mm = nc.tensor.matmul
        ACTV = nc.scalar.activation
        TT, TS, STT = nc.vector.tensor_tensor, nc.vector.tensor_scalar, nc.vector.scalar_tensor_tensor
        ident = C["ident"]

        h1 = ar(3 * D, "p (t d) -> p t d", t=3)
        mixer_floor = top[0]
        cst_a = ar(sum(n for _, n in CONSTS_A))
        at = 0
        for name, n in CONSTS_A:
            C[name] = cst_a[:, at:at + n]
            at += n
        uT = ar(KT * TOKS, "p (k t) -> p k t", k=KT)
        rqT = ar(H1 * TOKS, "p (h t) -> p h t", h=H1)
        rkT = ar(H1 * TOKS, "p (h t) -> p h t", h=H1)
        rv = ar(3 * 512, "p (t c) -> p t c", t=3)
        rg = ar(3 * 512, "p (t c) -> p t c", t=3)
        mv = ar(3 * H1 * 129, "p (t h c) -> p t h c", t=3, h=H1)
        mo = ar(3 * 512, "p (t c) -> p t c", t=3)
        CP = TOKS + 4
        conv_flat = ar(8 * CP)
        conv_in = conv_flat.rearrange("p (c t) -> p c t", c=8)
        gate_rows = conv_flat[0:4, 0:8 * TOKS].rearrange("p (r t) -> p r t", r=8)
        qkm = ar(8 * TOKS, "p (c t) -> p c t", c=8)
        heads_out = ar(2 * 3 * 512, "p (m t c) -> p m t c", m=2, t=3)
        xn = heads_out.rearrange("p m t c -> p (m t c)").rearrange("p (t d) -> p t d", t=3)
        work = ar(4 * 3 * TOKS)
        rot_in = work[:, 0:8 * TOKS].rearrange("p (h t) -> p h t", h=8)
        rot_part = [work[:, (8 + i) * TOKS:(9 + i) * TOKS] for i in range(2)]
        weights2 = [work[:, i * 3 * TOKS:(i + 1) * 3 * TOKS].rearrange("p (j t) -> p j t", j=3) for i in range(4)]
        yT = uT
        lgam = small[:, 1:9]
        tmp8 = small[:, 9:17]
        bias4 = small[0:4, 17:21]
        ss = small[:, 21:24]
        rstd = small[:, 24:27]
        st4 = small[:, 27:31]
        st4b = small[:, 31:35]
        den2 = small[:, 35:41]
        gate_cols = ar(3 * 16, "p (t c) -> p t c", t=3)
        wgate1 = ar(KT * 16, "p (k c) -> p k c", k=KT)
        prm_rows = [rot_in.rearrange("p h t -> p (h t)")[:, i * P:(i + 1) * P] for i in range(3)]

        norm_std_ready, xn_ready, xnT_ready, xnT_read = sem("norm_std_ready"), sem("xn_ready"), sem("xnT_ready"), sem("xnT_read")
        proj_ready, proj_read = sem("proj_ready"), sem("proj_read")
        conv_in_ready, conv_done = sem("conv_in_ready"), sem("conv_done")
        softplus_in, softplus_out = sem("softplus_in"), sem("softplus_out")
        products_ready, products_read = sem("products_ready"), sem("products_read")
        exps_asked, exps_ready = sem("exps_asked"), sem("exps_ready")
        masks_asked, masks_done = sem("masks_asked"), sem("masks_done")
        weights_ready, mixed_ready, mixed_read = sem("weights_ready"), sem("mixed_ready"), sem("mixed_read")
        pad_ready = sem("pad_ready")

        def transposed_norm_pe(pe, tiles, buf=xn):
            pe.wait_ge(xn_ready, due(pe, xn_ready))
            for k in range(KT):
                for t, (r, off) in enumerate(tiles):
                    last = nc.tensor.transpose(ps[k][:, off:off + r], buf[:r, t, k * P:(k + 1) * P], ident[:r, :r])
                last.then_inc(xnT_ready, up(xnT_ready))

        def norm_act(act, src, tiles, buf=xn):
            for t, (r, _) in enumerate(tiles):
                ACTV(buf[:r, t, :], src[:r, t, :], ACT.Square, accum_out=ss[:r, t:t + 1]).then_inc(act_order, up(act_order))
                act.wait_ge(act_order, own(act, act_order))
            for t, (r, _) in enumerate(tiles):
                ACTV(ss[:r, t:t + 1], ss[:r, t:t + 1], ACT.Sqrt, scale=1.0 / D, bias=eps_col[:r, :]).then_inc(norm_std_ready, up(norm_std_ready))
                act.wait_ge(norm_std_ready, own(act, norm_std_ready))

        def norm_dve(dve, src, tiles, dst=xn):
            for t, (r, _) in enumerate(tiles):
                dve.wait_ge(norm_std_ready, due(dve, norm_std_ready))
                nc.vector.reciprocal(rstd[:r, t:t + 1], ss[:r, t:t + 1]).then_inc(dve_order, up(dve_order))
                dve.wait_ge(dve_order, own(dve, dve_order))
                ins = TS(dst[:r, t, :], src[:r, t, :], rstd[:r, t:t + 1], None, ALU.mult)
                signal = xn_ready if t == len(tiles) - 1 else dve_order
                ins.then_inc(signal, up(signal))
                dve.wait_ge(signal, own(dve, signal))
        def by_feature(pe, base, views, x, n_toks):
            for half, (w, slot, count, _) in enumerate(views):
                pe.wait_ge(slot, count)
                kts = w.shape[1]
                for ct in range(w.shape[2] // P):
                    for k in range(kts):
                        last = mm(ps[base + ct][:, 0:n_toks], w[:, k, ct * P:(ct + 1) * P], x[:, half * kts + k, :],
                                  start=half + k == 0, stop=half == len(views) - 1 and k == kts - 1)
                last.then_inc(piece_used, up(piece_used))

        def by_token(pe, base, views, x, tiles):
            for half, (w, slot, count, _) in enumerate(views):
                pe.wait_ge(slot, count)
                kts = w.shape[1]
                for t, (r, off) in enumerate(tiles):
                    for k in range(kts):
                        last = mm(ps[base + t][:r, 0:w.shape[2]], x[:, half * kts + k, off:off + r], w[:, k, :],
                                  start=half + k == 0, stop=half == len(views) - 1 and k == kts - 1)
                last.then_inc(piece_used, up(piece_used))

        gates_w = A["w_in"]
        proj_pieces = [column_pieces(A["w_in"], g * 512, 512) for g in range(8)]
        ada_pieces = [column_pieces(A["ada_w_2"], g * 512, 512) for g in range(12)]
        ada_rows = arena[:, arena.shape[1] - 12 * SEQ:].rearrange("p (g c) -> p g c", g=12)
        sT = arena[:, arena.shape[1] - 12 * SEQ - 2 * KT:arena.shape[1] - 12 * SEQ].rearrange("p (k s) -> p k s", s=2)
        ada_copied, sT_ready = sem("ada_copied"), sem("sT_ready")
        ADA_STEPS = 6
        w_out_pieces = rows_pieces(A["w_out"])
        n_pieces_mixer = len(pieces)
        n_inputs_a = 2 + 2 + sum(len(b) for b in PARAMS) + 3
        lf_row, b_row = gate_rows[:, 6, :], gate_rows[:, 7, :]
        def g_row(d): return gate_rows[:, d, :]
        def m_row(d): return gate_rows[:, 2 + d, :]
        def em_row(d): return gate_rows[:, 4 + d, :]
        def timed(v, d):
            return v if d == 0 else v[:, ::-1]
        ones4 = C["ones"][0:4, 0:1].to_broadcast([4, TOKS])
        JOBS = [("mlstm", h) for h in range(H1)] + [("ret", h) for h in range(H1)]
        def reach(j, d):
            r, off = TILES[j]
            return (off, TOKS) if d == 0 else (0, off + r)
        NUM = 129
        sqrt_asked, sqrt_ready, heads_normed = sem("sqrt_asked"), sem("sqrt_ready"), sem("heads_normed")
        def rows_product(pe, views, xT, tiles, base=0):
            n = sum(w.shape[1] for w, _, _, _ in views)
            at = 0
            for w, slot, count, _ in views:
                pe.wait_ge(slot, count)
                for k in range(w.shape[1]):
                    for t, (r, off) in enumerate(tiles):
                        for half in range(2):
                            last = mm(ps[base + 2 * t + half][:r, :], xT[:, at, off:off + r],
                                      w[:, k, half * BANK:(half + 1) * BANK], start=at == 0, stop=at == n - 1)
                    at += 1
                last.then_inc(piece_used, up(piece_used))

        x_ready, cos_done = sem("x_ready"), sem("cos_done")
        top[0] = mixer_floor
        u2 = ar(3 * D, "p (t d) -> p t d", t=3)
        u2T = ar(KT * TOKS, "p (k t) -> p k t", k=KT)
        experts_floor = top[0]
        top[0] = mixer_floor
        hid = ar(FF)
        hidT = ar(FT * CAP, "p (f s) -> p f s", f=FT)
        x_cur = [ar(KT * CAP, "p (k s) -> p k s", k=KT) for _ in range(2)]
        top[0] = experts_floor
        xsT = ar((N_EXP + 2) * KT * CAP, "p (e k s) -> p e k s", e=N_EXP + 2, k=KT)
        y_all = ar(PAIRS * D, "p (i d) -> p i d", i=PAIRS)
        pgT = ar(PAIRS * TOKS, "p (i t) -> p i t", i=PAIRS)
        y_flat = y_all.rearrange("p i d -> p (i d)")
        onehot = y_flat[:, 0:3 * N_EXP * SLOT].rearrange("p (t e s) -> p t e s", t=3, e=N_EXP)
        weighted = y_flat[:, 3 * N_EXP * SLOT:6 * N_EXP * SLOT].rearrange("p (t e s) -> p t e s", t=3, e=N_EXP)
        w_router_sb = ar(KT * N_EXP, "p (k e) -> p k e", k=KT)
        aff = ar(3 * N_EXP, "p (t e) -> p t e", t=3)
        slots = ar(3 * N_EXP, "p (t e) -> p t e", t=3)
        rows16 = ar(5 * TOKS, "p (r t) -> p r t", r=5)[0:N_EXP]
        affT, left, chosen, tied, slot_row = (rows16[:, i, :] for i in range(5))
        top8 = small[0:N_EXP, 1:9]
        count1 = small[0:N_EXP, 9:10]
        mx3, sum3 = small[:, 10:13], small[:, 13:16]
        router_landed, logits_ready, exp_asked1, exp_ready1 = (sem(n) for n in ("router_landed", "logits_ready", "exp_asked1", "exp_ready1"))
        aff_ready, affT_ready, slots_ready, slotsT_ready = (sem(n) for n in ("aff_ready", "affT_ready", "slots_ready", "slotsT_ready"))
        onehot_ready, banks_filled, banks_read = sem("onehot_ready"), sem("banks_filled"), sem("banks_read")
        x_cur_ready, gate_done, hid_done, hid_turned, hidT_ready, y_read = (
            sem(n) for n in ("x_cur_ready", "gate_done", "hid_done", "hid_turned", "hidT_ready", "y_read"))
        down_done = sem("down_done")
        EXPERT_PIECES = 2 * KT + FT // 2
        LOOPS = PAIRS
        first_expert_piece = len(pieces)
        def loop_piece():
            n = len(pieces)
            k = n % RING
            slot_count[k] += 1
            pieces.append(None)
            return k, 16 * slot_count[k], n
        loop_pieces = [loop_piece() for _ in range(2 * EXPERT_PIECES)]
        SLOT_STEP = 16 * (2 * EXPERT_PIECES // RING)
        assert 2 * EXPERT_PIECES % RING == 0
        for k in range(RING):
            slot_count[k] += (LOOPS - 1) * SLOT_STEP // 16
        pieces += [None] * ((LOOPS - 1) * 2 * EXPERT_PIECES)
        HID_BANKS = [(c, c * BANK, min(BANK, FF - c * BANK)) for c in range(6)]
        TURNED = FT // 2
        PER = {"piece_used": 2 * EXPERT_PIECES, "x_cur_ready": 2, "gate_done": 10, "silu_done": 12, "hid_done": 12,
               "hid_turned": 4, "hidT_ready": 4, "y_read": 2}

        def after_piece(i, b, j):
            return i * PER["piece_used"] + first_expert_piece + b * EXPERT_PIECES + j + 1
        silu_done = sem("silu_done")
        def final_norm_act(act, src):
            norm_act(act, src, TILES2, u2)
        def final_norm_dve(dve, src, dst):
            norm_dve(dve, src, TILES2, u2)
            for t in range(2):
                signal = final_ready if t else dve_order
                TT(dst[:, t, :], u2[:, t, :], g_rows, ALU.mult).then_inc(signal, up(signal))
                dve.wait_ge(signal, own(dve, signal))
        g_rows = xsT.rearrange("p e k s -> p (e k s)")[:, 0:D]
        final_ready, g_rows_landed = sem("final_ready"), sem("g_rows_landed")
        x1 = h1[:, 1:3, :]
        N_PHASES_1 = 8
        phases_before_second = N_PHASES_1
        top[0] = 3 * D
        mods = ar(48 * 2, "p (j s) -> p j s", s=2)
        gains = ar(KT * 2, "p (k s) -> p k s", s=2)
        join = ar(14 * P, "p (s c) -> p s c", s=14)
        oaT = ar(4 * SEQ, "p (h t) -> p h t", h=4)
        obT = ar(4 * SEQ, "p (h t) -> p h t", h=4)
        u2x_lat = ar(KT * SEQ, "p (k t) -> p k t", k=KT)
        rwkv_floor = top[0]
        u2x_ctx = ar(KT * SEQ, "p (k t) -> p k t", k=KT)
        u2x_both = arena[:, rwkv_floor - KT * SEQ:rwkv_floor + KT * SEQ].rearrange("p (s k t) -> p k s t", s=2, k=KT)
        second_floor = top[0]
        c_rows = ar(2 * D, "p (t d) -> p t d", t=2)
        cn = ar(2 * D, "p (t d) -> p t d", t=2)
        second_landed, mods_ready = sem("second_landed"), sem("mods_ready")
        u2x_ready = sem("u2x_ready")
        N_PHASES_E = phases_before_second + 1
        mods_turned = sem("mods_turned")
        ORDER = [(0, 1, 2, 3), (1, 0, 3, 2)]
        TOKS2 = 2 * SEQ
        top[0] = second_floor
        CP2 = SEQ + 4
        gdn_in = [ar(4 * 2 * CP2, "p (c s t) -> p c s t", c=4, s=2) for _ in range(2)]
        vT = ar(4 * TOKS2, "p (h t) -> p h t", h=4)
        top[0] = second_floor
        wide4 = lambda: ar(4 * P, "p (h c) -> p h c", h=4)
        decayT, lT, attT, xm, xT_, p1, rhs, egrow = ([wide4() for _ in range(2)] for _ in range(8))
        kd, vnew, qd = decayT, p1, egrow
        assert top[0] >= second_floor + 2 * 4 * 2 * CP2 + 4 * TOKS2
        qT = ar(4 * SEQ, "p (h t) -> p h t", h=4)
        kT = ar(4 * TOKS2, "p (h t) -> p h t", h=4)
        k_tm = ar(4 * 512, "p (c h e) -> p c h e", c=4, h=4)
        vb = ar(2 * 4 * 512, "p (d c h e) -> p d c h e", d=2, c=4, h=4)
        zg = ar(2 * 512, "p (c f) -> p c f", c=2)
        oacc = ar(2 * 512, "p (c h e) -> p c h e", c=2, h=4)
        state = [wide4() for _ in range(2)]
        sq2 = ar(TOKS2)
        ab = ar(4 * 16, "p (c e) -> p c e", c=4)
        gcol = ar(4 * 8, "p (c e) -> p c e", c=4)
        beta = ar(4 * 8, "p (c e) -> p c e", c=4)
        gcum = ar(4 * 8, "p (c e) -> p c e", c=4)
        egb = ar(4 * 8, "p (c e) -> p c e", c=4)
        alog = ar(8)
        dtb = ar(8)
        wab = ar(KT * 16, "p (k c) -> p k c", k=KT)
        tmp32 = ar(4 * 8, "p (c e) -> p c e", c=4)
        kdecay, sdecay = ([ar(4) for _ in range(2)] for _ in range(2))
        gd_landed = sem("gd_landed")
        gdn_pieces = [column_pieces(A["w_in_2"], g * 512, 512) for g in (1, 2, 0, 3)]
        n_gdn = len(pieces)
        turned, turned_read, gdn_in_ready, pad_ready2 = sem("turned"), sem("turned_read"), sem("gdn_in_ready"), sem("pad_ready2")
        squared, normed_sum, root_ready = sem("squared"), sem("normed_sum"), sem("root_ready")
        gates_ready, act_asked, act_ready = sem("gates_ready"), sem("act_asked"), sem("act_ready")
        group_read, silu_asked, silu_ready, cums_ready = (sem(n) for n in ("group_read", "silu_asked", "silu_ready", "cums_ready"))
        g_products, decay_asked, decay_ready, x_ready2 = (
            sem(n) for n in ("g_products", "decay_asked", "decay_ready", "x_ready2"))
        step_filled, step_read, chunk_filled, chunk_read = (
            sem(n) for n in ("step_filled", "step_read", "chunk_filled", "chunk_read"))
        x_turned, x_copied, rhs_ready, new_filled, new_copied = (
            sem(n) for n in ("x_turned", "x_copied", "rhs_ready", "new_filled", "new_copied"))
        rhs_flat = gdn_in[0].rearrange("p c s t -> p (c s t)")[:, 0:TOKS2]
        LEVELS = (2, 4, 8, 16, 32, 64)

        def join_mask(level, d, transposed=False):
            lower = (d == 0) != transposed
            return join[:, (0 if lower else 7) + level, :].unsqueeze(1).to_broadcast([P, 4, P])

        def flat4h(v):
            return v.rearrange("p h c -> p (h c)")

        def bank4(b):
            return ps[b][:, :].rearrange("p (h c) -> p h c", h=4)

        per_head = lambda v: v.unsqueeze(2).to_broadcast([P, 4, P])
        C7, NC7, NCL = 64, 8, 4
        ORDER7 = [(0, 1, 2, 3, 4, 5, 6, 7), (3, 2, 1, 0, 7, 6, 5, 4)]
        KAPPA = float(np.exp(-0.5))
        ROWS7, COLS7 = SEQ // 64, 64
        yacc = h1[:, 0, :].rearrange("p (c q v) -> p c q v", c=NCL, q=4)
        top[0] = rwkv_floor
        r7_floor = top[0]
        by_pair = lambda t: ar(4 * t, "p (q t) -> p q t", q=4)
        kk7, k7 = by_pair(TOKS2), by_pair(TOKS2)
        r7, bonus = by_pair(SEQ), by_pair(SEQ)
        vlat7 = obT
        v7 = ar(NC7 * 4 * C7, "p (c q v) -> p c q v", c=NC7, q=4)
        wl, al, gl = ar(TOKS2), ar(TOKS2), ar(SEQ)
        al7, cs7, bt7, kt7 = (by_pair(TOKS2) for _ in range(4))
        rt7 = cs7[:, :, SEQ:]
        dmid, dend, dboth = (ar(4 * NC7, "p (q c) -> p q c", q=4) for _ in range(3))
        chunk_floor = top[0]
        w2sb, a2sb, e7 = ar(512), ar(512), by_pair(TOKS2)
        top[0] = chunk_floor
        spread = lambda: ar(4 * P, "p (q c) -> p q c", q=4)
        ax2, bx2, kx2, rx2 = ([spread() for _ in range(2)] for _ in range(4))
        l7, lk, ark, arb = (spread() for _ in range(4))
        xx = [ar(4 * P, "p (m q c) -> p m q c", m=2, q=2) for _ in range(2)]
        pp = [lk[:, 2 * g:2 * g + 2, :] for g in range(2)]
        u7 = ar(4 * C7, "p (q v) -> p q v", q=4)
        s7 = ar(4 * C7, "p (q v) -> p q v", q=4)
        sm7 = ar(4 * C7, "p (q v) -> p q v", q=4)
        u7t = pp[0][:, :, 0:P].rearrange("p i c -> p (i c)").rearrange("p (q v) -> p q v", q=4)
        top[0] = r7_floor + 2 * 4 * TOKS2 + 2 * 4 * SEQ + NC7 * 4 * C7 + 2 * TOKS2 + SEQ
        SP2 = SEQ + 2
        shift_in = [ar(4 * 2 * SP2, "p (c s t) -> p c s t", c=4, s=2) for _ in range(2)]
        vT7, t7 = by_pair(TOKS2), ar(TOKS2)
        rwkv_pieces = [column_pieces(A["w_in_2"], 2064 + g * 512, n) for g, n in ((1, 512), (2, 512), (0, 512), (3, 384))]
        n_rwkv = len(pieces)
        shift_ready, shift_read, w2_landed, k7_ready, sum7_ready, root7 = (
            sem(n) for n in ("shift_ready", "shift_read", "w2_landed", "k7_ready", "sum7_ready", "root7"))
        bonus7_ready = sem("bonus7_ready")
        pads7, lo_asked, lo_ready = sem("pads7"), sem("lo_asked"), sem("lo_ready")
        zw_ready, sig_ready, e7_asked, e7_ready, spread_ready = (
            sem(n) for n in ("zw_ready", "sig_ready", "e7_asked", "e7_ready", "spread_ready"))
        prod7, prod7_read, inv_filled, inv_read, inv_start = (
            sem(n) for n in ("prod7", "prod7_read", "inv_filled", "inv_read", "inv_start"))
        c7_filled, v7_filled = sem("c7_filled"), sem("v7_filled")

        def scan_order(v):
            return v.rearrange("p (w r) -> p r w", r=ROWS7)
        N_PHASES_R = N_PHASES_E + 3
        flat4 = lambda v: v.rearrange("p q t -> p (q t)")
        chunks = lambda v: v.rearrange("p q (c t) -> p q c t", t=C7)
        MID = C7 // 2

        def blocks(v, h):
            return v[C7 * h:C7 * (h + 1), :, C7 * h:C7 * (h + 1)]
        turned7, u7_filled, u7_copied = sem("turned7"), sem("u7_filled"), sem("u7_copied")
        chunk7_done, l7_ready = sem("chunk7_done"), sem("l7_ready")
        top[0] = chunk_floor
        g2sb = ar(512)
        yT7 = by_pair(SEQ)
        yb7 = ar(4 * C7, "p (q v) -> p q v", q=4)
        mean7, var7 = ar(4), ar(4)
        yx7 = spread()
        N_PHASES_R2 = N_PHASES_R + 4
        g2_landed, y7_ready, y7_read, gate7_ready = (sem(n) for n in ("g2_landed", "y7_ready", "y7_read", "gate7_ready"))
        lnx_eps = small[:, 47:48]
        A_COLS, B_COLS = 2064, 1920
        top[0] = rwkv_floor
        sgate = [ar(4 * SEQ, "p (c t) -> p c t", c=4) for _ in range(2)]
        term = ar(4 * SEQ, "p (c t) -> p c t", c=4)
        merged = ar(KT * SEQ, "p (k t) -> p k t", k=KT)
        mod_row = ar(D)
        merge_floor = top[0]
        MERGE = [(g, br) for g in range(2) for br in range(2)]
        merge_pieces = [column_pieces(A["w_in_2"], A_COLS + B_COLS + br * D + g * 512, 512)
                        + [piece((A["w_o_a_2"], A["w_o_b_2"])[br][:, g * 512:(g + 1) * 512].rearrange("(k p) c -> p k c", p=P),
                                 4 * 512, "p (k c) -> p k c", {"k": 4})] for g, br in MERGE]
        w_out2_pieces = rows_pieces(A["w_out_2"])
        n_merge = len(pieces)
        sgate_ready, merge_read, m_row_filled, m_row_read = (
            sem(n) for n in ("sgate_ready", "merge_read", "m_row_filled", "m_row_read"))
        top[0] = rwkv_floor
        N_GRP, PER_GRP = 4, 8
        N_EXP2, DE = N_GRP * PER_GRP, 256
        xn2 = ar(2 * D, "p (t d) -> p t d", t=2)
        m5_row = ar(D)
        g_out = ar(D)
        hidb = [ar(2 * SEQ, "p (f t) -> p f t", f=2) for _ in range(2)]
        upb = [ar(2 * SEQ, "p (f t) -> p f t", f=2) for _ in range(2)]
        combB = ar(N_EXP2 * SEQ, "p (e t) -> p e t", e=N_EXP2)
        LG = N_GRP + N_EXP2
        router_w = ar(KT * LG, "p (k e) -> p k e", k=KT)
        router_b = ar(LG)
        zeros1 = ar(P)
        gains2 = ar(KT)
        combT = ar(SEQ)
        logits = ar(2 * LG, "p (t e) -> p t e", t=2)
        comb = ar(2 * N_EXP2, "p (t g e) -> p t g e", t=2, g=N_GRP)
        gp, gsel, gcnt = (ar(2 * N_GRP, "p (t g) -> p t g", t=2) for _ in range(3))
        ing, rest, sel1, sel2, ecnt = (ar(2 * PER_GRP, "p (t e) -> p t e", t=2) for _ in range(5))
        gmax, psel, max1, max2, wt1, wt2 = (ar(2) for _ in range(6))
        tT = u2x_lat
        N_PHASES_M = N_PHASES_R2 + 2
        moe_landed, tT_ready, logits2_ready, e2_asked, e2_ready, comb_ready, combT_read = (
            sem(n) for n in ("moe_landed", "tT_ready", "logits2_ready", "e2_asked", "e2_ready", "comb_ready", "combT_read"))
        spread_filled, spread_read, silu2_ready, hid2_ready, m5_ready = (
            sem(n) for n in ("spread_filled", "spread_read", "silu2_ready", "hid2_ready", "m5_ready"))

        def moe_piece(e, which):
            w = (A["moe_w_gate_2"], A["moe_w_up_2"], A["moe_w_down_2"])[which].rearrange("g e k f -> (g e) k f")
            return w[bass.ds(e, 1), :, :].rearrange("o (k p) c -> p (o k) c", p=P)

        def moe_view(n):
            return ring[:, n % RING * PIECE:n % RING * PIECE + 2048]

        moe_first = len(pieces)
        MOE_LOOPS = N_EXP2 // 2 - 1
        assert RING == 6
        moe_count = {n: 16 * (slot_count[n % RING] + 1 + (n - moe_first) // RING) for n in range(moe_first, moe_first + 3 * N_EXP2)}
        PER2 = {"piece_used": 6, "silu2_ready": 2, "hid2_ready": 2, "dve_order": 2}
        LOOP0, TAIL = moe_first + 2, moe_first + 2 + 6 * MOE_LOOPS
        summed_ready, out_ready = sem("summed_ready"), sem("out_ready")
        block = ctx.enter_context(nc.Block())

        @block.sync
        def _(sp):
            def load(dst, src):
                sp.dma_start(dst, src).then_inc(inputs_landed, up(inputs_landed, 16))

            load(h1[0:N_META, 0, :], A["meta_tokens"])
            load(h1[:, 1:3, :], A["x"].rearrange("(t p) d -> p t d", p=P))
            load(cst_all[:, :], consts[0])
            load(cst_a, consts[1])
            for rows, batch in zip(prm_rows, PARAMS):
                r = 0
                for name, n in batch:
                    src = A[name]
                    src = src.rearrange("a b -> (a b)") if len(src.shape) == 2 else src
                    load(rows[r:r + n, :], src.rearrange("(r c) -> r c", c=P))
                    r += n
            load(wgate1, A["w_in"][:, 4096:4112].rearrange("(k p) c -> p k c", p=P))
            load(lgam, A["ret_decay_logit"].rearrange("a b -> (a b)").partition_broadcast(P))
            with nc.allow_non_contiguous_dma(reason="sixteen biases"):
                load(bias4, A["b_gates"].rearrange("(q h) -> h q", h=4))
            n_inputs = given["inputs_landed"]

            def issue(lo, hi):
                for n in range(lo, hi):
                    src, view, k, _ = pieces[n]
                    if n >= RING:
                        sp.wait_ge(piece_used, n - RING + 1)
                    sp.dma_start(view, src).then_inc(landed[k], 16)

            issue(0, n_pieces_mixer)
            sp.wait_ge(phase_ended, 20)
            sp.dma_start(w_router_sb, A["w_router"].rearrange("(k p) e -> p k e", p=P)).then_inc(router_landed, up(router_landed, 16))
            def dram_piece(e, j):
                if j < 2 * KT:
                    w = A["w_gate" if j % 2 == 0 else "w_up"]
                    return w[bass.ds(e, 1), j // 2 * P:(j // 2 + 1) * P, :].rearrange("o p c -> p (o c)"), FF
                f = 2 * (j - 2 * KT)
                return A["w_down"][bass.ds(e, 1), f * P:(f + 2) * P, :].rearrange("o (k p) c -> p (o k) c", p=P), 2 * D

            with looped(sp, LOOPS, PER) as i:
                for b in range(2):
                    for j in range(EXPERT_PIECES):
                        k, _, n = loop_pieces[b * EXPERT_PIECES + j]
                        src, floats = dram_piece(2 * i + b, j)
                        view = ring[:, k * PIECE:k * PIECE + floats]
                        if j >= 2 * KT:
                            view = view.rearrange("p (k c) -> p k c", k=2)
                        sp.wait_ge(piece_used, i * PER["piece_used"] + n - RING + 1)
                        sp.dma_start(view, src).then_inc(landed[k], 16)
            sp.wait_ge(phase_ended, N_PHASES_1 * 4)
            sp.dma_start(g_rows, A["final_norm_g"].partition_broadcast(P)).then_inc(g_rows_landed, up(g_rows_landed, 16))
            sp.wait_ge(final_ready, due(sp, final_ready))
            for dst, src in ((join.rearrange("p s c -> p (s c)"), consts[2]),
                             (c_rows, A["ctx_2"].rearrange("(t p) d -> p t d", p=P))):
                sp.dma_start(dst, src).then_inc(second_landed, up(second_landed, 16))
            sp.wait_ge(phase_ended, 4 * N_PHASES_E)
            for dst, src in ((alog, A["gdn_a_log_2"].rearrange("a b -> (a b)").partition_broadcast(P)),
                             (dtb, A["gdn_dt_bias_2"].rearrange("a b -> (a b)").partition_broadcast(P)),
                             (wab, A["w_in_2"][:, 2048:2064].rearrange("(k p) c -> p k c", p=P))):
                sp.dma_start(dst, src).then_inc(gd_landed, up(gd_landed, 16))
            issue(n_gdn - 8, n_gdn)
            issue(n_rwkv - 8, n_rwkv)
            for d in range(2):
                sp.wait_ge(phase_ended, 4 * (N_PHASES_R + 2 * d))
                for dst, src in ((w2sb, A["rwkv_w2_2"]), (a2sb, A["rwkv_a2_2"])):
                    sp.dma_start(dst, src.rearrange("d r c -> (d r) c")).then_inc(w2_landed, up(w2_landed, 16))
            sp.wait_ge(phase_ended, 4 * N_PHASES_R2)
            sp.dma_start(g2sb, A["rwkv_g2_2"]).then_inc(g2_landed, up(g2_landed, 16))
            issue(n_merge - 16, n_merge)
            sp.wait_ge(phase_ended, 4 * N_PHASES_M)
            for dst, src in ((router_w[:, :, 0:N_GRP], A["router_grp_2"].rearrange("(k p) e -> p k e", p=P)),
                             (router_w[:, :, N_GRP:LG], A["router_exp_2"].rearrange("(k p) e -> p k e", p=P)),
                             (router_b[:, 0:N_GRP], A["router_grp_b_2"].partition_broadcast(P)),
                             (router_b[:, N_GRP:LG], A["router_exp_b_2"].partition_broadcast(P)),
                             (g_out, A["final_norm_g_2"].partition_broadcast(P))):
                sp.dma_start(dst, src).then_inc(moe_landed, up(moe_landed, 16))

            def moe_issue(n, e, which, i=0):
                sp.wait_ge(piece_used, 6 * i + n - RING + 1)
                sp.dma_start(moe_view(n).rearrange("p (k c) -> p k c", k=2 if which == 2 else KT),
                             moe_piece(e, which)).then_inc(landed[n % RING], 16)

            for which in range(2):
                moe_issue(moe_first + which, 0, which)
            with sp.Fori(0, MOE_LOOPS) as i:
                for j, (e, which) in enumerate(((1, 0), (1, 1), (0, 2), (2, 0), (2, 1), (1, 2))):
                    moe_issue(LOOP0 + j, 2 * i + e, which, i)
            for j, (e, which) in enumerate(((31, 0), (31, 1), (30, 2), (31, 2))):
                moe_issue(TAIL + j, e, which)
            for t in range(2):
                sp.wait_ge(out_ready, due(sp, out_ready))
                sp.dma_start(out[t * P:(t + 1) * P, :], xn2[:, t, :]).then_inc(out_written, up(out_written, 16))
            sp.wait_ge(out_written, 32)

        @block.gpsimd
        def _(pool):
            pool.drain().then_inc(phase_ended, 1)
            pool.wait_ge(phase_ended, phase_end(pool))
            pool.drain().then_inc(phase_ended, 1)
            pool.wait_ge(phase_ended, phase_end(pool))

            for i in range(8):
                kind = "q" if i < 4 else ""
                dst = (rqT if i < 4 else rkT)[:, i % 4, :]
                nc.gpsimd.tensor_tensor(dst, rot_in[:, i, :], C["cos" + kind], ALU.mult).then_inc(cos_done, up(cos_done))
                pool.wait_ge(cos_done, own(pool, cos_done))
            pool.drain().then_inc(phase_ended, 1)
            pool.wait_ge(phase_ended, phase_end(pool))
            for n, (kind, h) in enumerate(JOBS):
                for d in range(2 if kind == "mlstm" else 0):
                    for j, (r, off) in enumerate(TILES):
                        w = weights2[2 * (n % 2) + d][:r, j, off:off + r]
                        pool.wait_ge(masks_asked, due(pool, masks_asked))
                        nc.gpsimd.tensor_tensor(w, w, C["tri_le" if d == 0 else "tri_ge"][:r, :r], ALU.mult).then_inc(masks_done, up(masks_done))
                        pool.wait_ge(masks_done, own(pool, masks_done))
            pool.drain().then_inc(phase_ended, 1)
            pool.wait_ge(phase_ended, phase_end(pool))
            pool.drain().then_inc(phase_ended, 1)
            pool.wait_ge(phase_ended, phase_end(pool))
            pool.drain().then_inc(phase_ended, 1)
            pool.wait_ge(phase_ended, phase_end(pool))
            nc.gpsimd.memset(y_flat[:, :], 0.0).then_inc(pool_order, up(pool_order))
            pool.wait_ge(pool_order, own(pool, pool_order))
            nc.gpsimd.memset(xsT[:, N_EXP:N_EXP + 2], 0.0).then_inc(pool_order, up(pool_order))
            pool.wait_ge(pool_order, own(pool, pool_order))
            for b in range(2):
                nc.gpsimd.tensor_copy(x_cur[b], xsT[:, b]).then_inc(x_cur_ready, up(x_cur_ready))
                pool.wait_ge(x_cur_ready, own(pool, x_cur_ready))
            pool.drain().then_inc(phase_ended, 1)
            pool.wait_ge(phase_ended, phase_end(pool))
            with looped(pool, LOOPS, PER) as i:
                for b in range(2):
                    pool.wait_ge(piece_used, after_piece(i, b, 2 * KT - 1))
                    nc.gpsimd.tensor_copy(x_cur[b].unsqueeze(1), xsT[:, bass.ds(2 * i + b + 2, 1)]).then_inc(x_cur_ready, up(x_cur_ready))
            pool.drain().then_inc(phase_ended, 1)
            pool.wait_ge(phase_ended, phase_end(pool))
            pool.drain().then_inc(phase_ended, 1)
            pool.wait_ge(phase_ended, phase_end(pool))

            pool.drain().then_inc(phase_ended, 1)
            pool.wait_ge(phase_ended, phase_end(pool))
            pool.drain().then_inc(phase_ended, 1)
            pool.wait_ge(phase_ended, phase_end(pool))

            pool.drain().then_inc(phase_ended, 1)
            pool.wait_ge(phase_ended, phase_end(pool))
            for d in range(2):
                pool.drain().then_inc(phase_ended, 1)
                pool.wait_ge(phase_ended, phase_end(pool))
                for v in (*ax2, *bx2, *kx2, *rx2):
                    nc.gpsimd.memset(v, 0.0).then_inc(pool_order, up(pool_order))
                    pool.wait_ge(pool_order, own(pool, pool_order))
                for n, c in enumerate(ORDER7[d]):
                    if n >= 2:
                        pool.wait_ge(chunk7_done, due(pool, chunk7_done))
                    for x2, v in ((ax2, al7), (bx2, bt7), (kx2, kt7), (rx2, rt7)):
                        x = x2[n % 2]
                        if x2 is rx2 and c < NCL:
                            continue
                        at = (c - NCL if x2 is rx2 else c) * C7
                        for h in range(2):
                            last = nc.gpsimd.tensor_copy(blocks(x, h), v[C7 * h:C7 * (h + 1), :, at:at + C7])
                            if h == 0:
                                last.then_inc(pool_order, up(pool_order))
                                pool.wait_ge(pool_order, own(pool, pool_order))
                        last.then_inc(spread_ready, up(spread_ready))
                        pool.wait_ge(spread_ready, own(pool, spread_ready))
                pool.wait_ge(chunk7_done, due(pool, chunk7_done, 2))
                pool.drain().then_inc(phase_ended, 1)
                pool.wait_ge(phase_ended, phase_end(pool))
            pool.drain().then_inc(phase_ended, 1)
            pool.wait_ge(phase_ended, phase_end(pool))

            pool.drain().then_inc(phase_ended, 1)
            pool.wait_ge(phase_ended, phase_end(pool))

        @block.scalar
        def _(act):
            act.wait_ge(inputs_landed, due(act, inputs_landed, 16 * n_inputs_a))
            act.wait_ge(pad_ready, due(act, pad_ready))
            norm_act(act, h1, TILES)
            ACTV(tmp8, lgam, ACT.Abs).then_inc(act_order, up(act_order))
            act.wait_ge(act_order, own(act, act_order))
            ACTV(tmp8, tmp8, ACT.Exp, scale=-1.0).then_inc(act_order, up(act_order))
            act.wait_ge(act_order, own(act, act_order))
            ACTV(tmp8, tmp8, ACT.Ln, bias=1.0).then_inc(softplus_out, up(softplus_out))
            act.wait_ge(softplus_out, own(act, softplus_out))
            act.drain().then_inc(phase_ended, 1)
            act.wait_ge(phase_ended, phase_end(act))
            for g in range(8):
                act.wait_ge(piece_used, after(proj_pieces[g]))
                base = 4 * (g % 2)
                if g in (0, 1):
                    for ct in range(4):
                        last = ACTV(rot_in[:, 4 * g + ct, :], ps[base + ct][:, 0:TOKS], ACT.Copy)
                elif g in (4, 5):
                    for ct in range(4):
                        last = ACTV(conv_in[:, 4 * (g - 4) + ct, 2:2 + TOKS], ps[base + ct][:, 0:TOKS], ACT.Copy)
                else:
                    for t, (r, _) in enumerate(TILES):
                        if g == 6:
                            last = ACTV(mv[:r, t, :, 0:P], ps[base + t][:r, :].rearrange("p (h c) -> p h c", h=H1), ACT.Copy)
                        else:
                            last = ACTV({2: rv, 3: rg, 7: mo}[g][:r, t, :], ps[base + t][:r, :],
                                        {2: ACT.Copy, 3: ACT.Silu, 7: ACT.Sigmoid}[g])
                last.then_inc(proj_read, up(proj_read))
                act.wait_ge(proj_read, own(act, proj_read))
            for c in range(8):
                act.wait_ge(conv_in_ready, due(act, conv_in_ready))
                ACTV(qkm[:, c, :], qkm[:, c, :], ACT.Silu).then_inc(act_order, up(act_order))
                act.wait_ge(act_order, own(act, act_order))
            for d in range(2):
                act.wait_ge(softplus_in, due(act, softplus_in))
                ACTV(em_row(d), lf_row, ACT.Abs).then_inc(act_order, up(act_order))
                act.wait_ge(act_order, own(act, act_order))
                ACTV(em_row(d), em_row(d), ACT.Exp, scale=-1.0).then_inc(act_order, up(act_order))
                act.wait_ge(act_order, own(act, act_order))
                ACTV(em_row(d), em_row(d), ACT.Ln, bias=1.0).then_inc(softplus_out, up(softplus_out))
                act.wait_ge(softplus_out, own(act, softplus_out))
                act.wait_ge(softplus_in, due(act, softplus_in))
                ACTV(em_row(d), em_row(d), ACT.Exp, scale=-1.0).then_inc(act_order, up(act_order))
                act.wait_ge(act_order, own(act, act_order))
            act.drain().then_inc(phase_ended, 1)
            act.wait_ge(phase_ended, phase_end(act))
            act.drain().then_inc(phase_ended, 1)
            act.wait_ge(phase_ended, phase_end(act))
            for s, name in enumerate(("c_2", "c_ctx_2")):
                last = ACTV(sT[:, :, s], prm[:, PCOL[name]:PCOL[name] + KT], ACT.Silu)
            last.then_inc(sT_ready, up(sT_ready))
            act.wait_ge(sT_ready, own(act, sT_ready))
            for n, (kind, h) in enumerate(JOBS):
                for d in range(2 if kind == "mlstm" else 1):
                    for j, (r, off) in enumerate(TILES):
                        c0, c1 = reach(j, d) if kind == "mlstm" else (0, TOKS)
                        w = weights2[2 * (n % 2) + d][:r, j, c0:c1]
                        act.wait_ge(exps_asked, due(act, exps_asked))
                        ACTV(w, w, ACT.Exp, scale=-1.0 if kind == "mlstm" else 1.0).then_inc(exps_ready, up(exps_ready))
                        act.wait_ge(exps_ready, own(act, exps_ready))
                if 1 <= n <= ADA_STEPS:
                    act.wait_ge(piece_used, after(ada_pieces[2 * n - 1]))
                    for u in range(2):
                        rows = slice(64 * u, 64 * u + 2)
                        last = ACTV(ada_rows[rows, 2 * n - 2:2 * n, :].rearrange("p g c -> p (g c)"), ps[7][rows, :], ACT.Copy)
                    last.then_inc(ada_copied, up(ada_copied))
                    act.wait_ge(ada_copied, own(act, ada_copied))
            act.drain().then_inc(phase_ended, 1)
            act.wait_ge(phase_ended, phase_end(act))
            for m in range(2):
                for t, (r, _) in enumerate(TILES):
                    act.wait_ge(sqrt_asked, due(act, sqrt_asked))
                    ACTV(st4b[:r], st4b[:r], ACT.Sqrt, scale=1.0 / P, bias=eps_col[:r]).then_inc(sqrt_ready, up(sqrt_ready))
                    act.wait_ge(sqrt_ready, own(act, sqrt_ready))

            act.drain().then_inc(phase_ended, 1)
            act.wait_ge(phase_ended, phase_end(act))
            norm_act(act, h1, TILES, u2)
            for t, (r, _) in enumerate(TILES):
                act.wait_ge(exp_asked1, due(act, exp_asked1))
                ACTV(aff[:r, t, :], aff[:r, t, :], ACT.Exp, bias=mx3[:r, t:t + 1], accum_out=sum3[:r, t:t + 1]).then_inc(exp_ready1, up(exp_ready1))
                act.wait_ge(exp_ready1, own(act, exp_ready1))
            act.drain().then_inc(phase_ended, 1)
            act.wait_ge(phase_ended, phase_end(act))
            act.drain().then_inc(phase_ended, 1)
            act.wait_ge(phase_ended, phase_end(act))
            act.drain().then_inc(y_read, up(y_read))
            with looped(act, LOOPS, PER) as i:
                for b in range(2):
                    for c, at, n in HID_BANKS:
                        if c < 5:
                            act.wait_ge(gate_done, due(act, gate_done))
                        else:
                            act.wait_ge(piece_used, after_piece(i, b, 2 * KT - 1))
                        ACTV(hid[0:CAP, at:at + n], ps[c][0:CAP, 0:n], ACT.Silu).then_inc(silu_done, up(silu_done))
                    act.wait_ge(piece_used, after_piece(i, b, EXPERT_PIECES - 1))
                    for half in range(2):
                        last = ACTV(y_all[SLOT * b:SLOT * b + CAP, bass.ds(i, 1), half * BANK:(half + 1) * BANK],
                                    ps[6][SLOT * half:SLOT * half + CAP, :].unsqueeze(1), ACT.Copy)
                    last.then_inc(y_read, up(y_read))
            act.drain().then_inc(phase_ended, 1)
            act.wait_ge(phase_ended, phase_end(act))
            final_norm_act(act, x1)
            act.wait_ge(second_landed, due(act, second_landed, 32))
            act.wait_ge(mods_ready, due(act, mods_ready))
            norm_act(act, c_rows, TILES2, cn)
            act.wait_ge(u2x_ready, due(act, u2x_ready, 8))
            norm_act(act, x1, TILES2, cn)
            act.drain().then_inc(phase_ended, 1)
            act.wait_ge(phase_ended, phase_end(act))
            act.wait_ge(pad_ready2, due(act, pad_ready2))
            for n in range(4):
                act.wait_ge(piece_used, after(gdn_pieces[n]))
                base = 4 * (n % 2)
                if n < 2:
                    for ct in range(4):
                        for s in range(2):
                            last = ACTV(gdn_in[n][:, ct, s, 2:2 + SEQ], ps[base + ct][:, (1 - s) * SEQ:(2 - s) * SEQ], ACT.Copy)
                elif n == 2:
                    act.wait_ge(gdn_in_ready, due(act, gdn_in_ready))
                    for ct in range(4):
                        last = ACTV(gdn_in[0][:, ct, 1, 2:2 + SEQ], ps[base + ct][:, 0:SEQ], ACT.Copy)
                else:
                    for t in range(2):
                        last = ACTV(zg[:, t, :], ps[base + t][:, :], ACT.Silu)
                last.then_inc(group_read, up(group_read))
                act.wait_ge(group_read, own(act, group_read))
                if n < 3:
                    dst = (kT, vT, qT)[n]
                    act.wait_ge(silu_asked, due(act, silu_asked))
                    ACTV(dst, dst, ACT.Silu).then_inc(silu_ready, up(silu_ready))
                    act.wait_ge(silu_ready, own(act, silu_ready))
            act.wait_ge(act_asked, due(act, act_asked))
            ACTV(beta, ab[:, :, 8:16], ACT.Sigmoid).then_inc(act_order, up(act_order))
            act.wait_ge(act_order, own(act, act_order))
            ACTV(tmp32, ab[:, :, 0:8], ACT.Abs).then_inc(act_order, up(act_order))
            act.wait_ge(act_order, own(act, act_order))
            ACTV(tmp32, tmp32, ACT.Exp, scale=-1.0).then_inc(act_order, up(act_order))
            act.wait_ge(act_order, own(act, act_order))
            ACTV(alog, alog, ACT.Exp).then_inc(act_order, up(act_order))
            act.wait_ge(act_order, own(act, act_order))
            ACTV(tmp32, tmp32, ACT.Ln, bias=1.0).then_inc(act_ready, up(act_ready))
            act.wait_ge(act_ready, own(act, act_ready))
            act.wait_ge(act_asked, due(act, act_asked))
            ACTV(egb, gcum, ACT.Exp).then_inc(act_ready, up(act_ready))
            act.wait_ge(act_ready, own(act, act_ready))
            for n in range(8):
                act.wait_ge(normed_sum, due(act, normed_sum))
                r = rhs_flat[:, 0:TOKS2 if n < 4 else SEQ]
                ACTV(r, ps[2 + n % 2][:, 0:r.shape[1]], ACT.Sqrt, bias=eps_col).then_inc(root_ready, up(root_ready))
                act.wait_ge(root_ready, own(act, root_ready))
            act.drain().then_inc(phase_ended, 1)
            act.wait_ge(phase_ended, phase_end(act))
            for p in range(4):
                for d in range(2):
                    act.wait_ge(decay_asked, due(act, decay_asked))
                    end = P - 1 if d == 0 else 0
                    ACTV(egrow[d], bank4(4 * d), ACT.Exp)
                    ACTV(sdecay[d].unsqueeze(2), bank4(4 * d)[:, :, end:end + 1], ACT.Exp)
                    ACTV(decayT[d], decayT[d], ACT.Exp).then_inc(decay_ready, up(decay_ready))
                    act.wait_ge(decay_ready, own(act, decay_ready))
                for d in range(2):
                    act.wait_ge(x_turned, due(act, x_turned))
                    ACTV(flat4h(xm[d]), ps[4 * d + 2][:, :], ACT.Copy).then_inc(x_copied, up(x_copied))
                    act.wait_ge(x_copied, own(act, x_copied))
                for d in range(2):
                    act.wait_ge(new_filled, due(act, new_filled))
                    ACTV(flat4h(vnew[d]), ps[4 * d][:, :], ACT.Copy).then_inc(new_copied, up(new_copied))
                    act.wait_ge(new_copied, own(act, new_copied))
            for t in range(2):
                act.wait_ge(sqrt_asked, due(act, sqrt_asked))
                ACTV(kdecay[0], kdecay[0], ACT.Sqrt, scale=1.0 / P, bias=eps_col).then_inc(sqrt_ready, up(sqrt_ready))
                act.wait_ge(sqrt_ready, own(act, sqrt_ready))
            act.drain().then_inc(phase_ended, 1)
            act.wait_ge(phase_ended, phase_end(act))
            act.wait_ge(pads7, due(act, pads7))
            for n in range(4):
                act.wait_ge(piece_used, after(rwkv_pieces[n]))
                base = 4 * (n % 2)
                if n >= 2:
                    act.wait_ge(shift_read, due(act, shift_read))
                for ct in range(4 if n < 3 else 3):
                    dst = shift_in[n % 2][:, ct, :, 1:1 + SEQ]
                    last = ACTV(scan_order(dst[:, 1]), ps[base + ct][:, 0:SEQ].rearrange("p (r w) -> p r w", r=ROWS7), ACT.Copy)
                    if n != 2:
                        last = ACTV(dst[:, 0], ps[base + ct][:, SEQ:TOKS2], ACT.Copy)
                last.then_inc(shift_ready, up(shift_ready))
                act.wait_ge(shift_ready, own(act, shift_ready))
            act.wait_ge(lo_asked, due(act, lo_asked))
            ACTV(wl, wl, ACT.Tanh).then_inc(act_order, up(act_order))
            act.wait_ge(act_order, own(act, act_order))
            ACTV(gl, gl, ACT.Sigmoid).then_inc(lo_ready, up(lo_ready))
            act.wait_ge(lo_ready, own(act, lo_ready))
            for q in range(4):
                act.wait_ge(sum7_ready, due(act, sum7_ready))
                ACTV(t7, ps[0][:, :], ACT.Sqrt, bias=eps_col).then_inc(root7, up(root7))
                act.wait_ge(root7, own(act, root7))
            act.drain().then_inc(phase_ended, 1)
            act.wait_ge(phase_ended, phase_end(act))
            for d in range(2):
                act.wait_ge(zw_ready, due(act, zw_ready))
                for q in range(4):
                    ACTV(al7[:, q, :], ps[q][:, :], ACT.Sigmoid, bias=pc("rwkv_w0_2", 4 * d + q))
                    last = ACTV(bt7[:, q, :], ps[4 + q][:, :], ACT.Sigmoid, bias=pc("rwkv_a0_2", 4 * d + q))
                last.then_inc(sig_ready, up(sig_ready))
                act.wait_ge(sig_ready, own(act, sig_ready))
                act.wait_ge(e7_asked, due(act, e7_asked))
                ACTV(flat4(e7), flat4(cs7), ACT.Exp, scale=KAPPA).then_inc(act_order, up(act_order))
                act.wait_ge(act_order, own(act, act_order))
                ACTV(flat4(al7), flat4(al7), ACT.Exp, scale=-KAPPA)
                for v in (dmid, dend, dboth):
                    ACTV(v, v, ACT.Exp, scale=-KAPPA)
                ACTV(rt7, rt7, ACT.Exp, scale=-KAPPA).then_inc(e7_ready, up(e7_ready))
                act.wait_ge(e7_ready, own(act, e7_ready))
                act.drain().then_inc(phase_ended, 1)
                act.wait_ge(phase_ended, phase_end(act))
                for n, c in enumerate(ORDER7[d]):
                    act.wait_ge(prod7, due(act, prod7))
                    ACTV(flat4(l7), ps[0][:, :], ACT.Copy).then_inc(l7_ready, up(l7_ready))
                    act.wait_ge(l7_ready, own(act, l7_ready))
                    act.wait_ge(turned7, due(act, turned7))
                    ACTV(flat4(bx2[n % 2]), ps[6][:, :], ACT.Copy, scale=-1.0)
                    ACTV(flat4(kx2[n % 2]), ps[7][:, :], ACT.Copy)
                    for b in (4, 5):
                        act.wait_ge(u7_filled, due(act, u7_filled))
                        ACTV(flat4(u7), ps[b][:, 0:4 * C7], ACT.Copy).then_inc(u7_copied, up(u7_copied))
                        act.wait_ge(u7_copied, own(act, u7_copied))
                act.drain().then_inc(phase_ended, 1)
                act.wait_ge(phase_ended, phase_end(act))
            for c in range(NCL):
                act.wait_ge(sqrt_asked, due(act, sqrt_asked))
                ACTV(var7, var7, ACT.Sqrt, scale=1.0 / C7, bias=lnx_eps).then_inc(sqrt_ready, up(sqrt_ready))
                act.wait_ge(sqrt_ready, own(act, sqrt_ready))
            act.drain().then_inc(phase_ended, 1)
            act.wait_ge(phase_ended, phase_end(act))
            for n in range(4):
                act.wait_ge(piece_used, after(merge_pieces[n][:2]))
                if n >= 2:
                    act.wait_ge(merge_read, due(act, merge_read))
                for b in range(2):
                    last = ACTV(sgate[n % 2][:, 2 * b:2 * b + 2, :].rearrange("p c t -> p (c t)"), ps[4 * (n % 2) + b][:, :], ACT.Sigmoid)
                last.then_inc(sgate_ready, up(sgate_ready))
                act.wait_ge(sgate_ready, own(act, sgate_ready))
            act.wait_ge(m_row_filled, due(act, m_row_filled))
            for b in range(2):
                last = ACTV(mod_row[:, b * BANK:(b + 1) * BANK], ps[4 + b][:, :], ACT.Copy)
            last.then_inc(m_row_read, up(m_row_read))
            act.wait_ge(m_row_read, own(act, m_row_read))
            act.drain().then_inc(phase_ended, 1)
            act.wait_ge(phase_ended, phase_end(act))
            norm_act(act, x1, TILES2, xn2)
            act.wait_ge(m_row_filled, due(act, m_row_filled))
            for b in range(2):
                last = ACTV(m5_row[:, b * BANK:(b + 1) * BANK], ps[2 + b][:, :], ACT.Copy)
            last.then_inc(m5_ready, up(m5_ready))
            act.wait_ge(m5_ready, own(act, m5_ready))
            act.wait_ge(e2_asked, due(act, e2_asked))
            ACTV(gp, gp, ACT.Exp).then_inc(e2_ready, up(e2_ready))
            act.wait_ge(e2_ready, own(act, e2_ready))
            act.wait_ge(e2_asked, due(act, e2_asked))
            ACTV(wt2, wt2, ACT.Exp).then_inc(e2_ready, up(e2_ready))
            act.wait_ge(e2_ready, own(act, e2_ready))
            act.wait_ge(spread_filled, due(act, spread_filled))
            for n in range(N_EXP2 // 2):
                act.wait_ge(spread_filled, due(act, spread_filled))
                ACTV(combB[:, 2 * n:2 * n + 2, :].rearrange("p e t -> p (e t)"), ps[4 + n % 4][:, :], ACT.Copy).then_inc(spread_read, up(spread_read))
                act.wait_ge(spread_read, own(act, spread_read))
            def moe_silu(b, n, i=0):
                act.wait_ge(piece_used, 6 * i + n + 1)
                ACTV(hidb[b].rearrange("p f t -> p (f t)"), ps[4 + 2 * b][:, :], ACT.Silu).then_inc(silu2_ready, up(silu2_ready))

            moe_silu(0, moe_first)
            with looped(act, MOE_LOOPS, PER2) as i:
                moe_silu(1, LOOP0, i)
                moe_silu(0, LOOP0 + 3, i)
            moe_silu(1, TAIL)
            act.wait_ge(summed_ready, due(act, summed_ready))
            norm_act(act, x1, TILES2, xn2)

        @block.vector
        def _(dve):
            nc.vector.memset(eps_col, EPS).then_inc(dve_order, up(dve_order))
            dve.wait_ge(dve_order, own(dve, dve_order))
            nc.vector.memset(small[:, 47:48], 1e-5 * 64).then_inc(dve_order, up(dve_order))
            dve.wait_ge(dve_order, own(dve, dve_order))
            nc.vector.memset(mv[:, :, :, 128:129], 1.0).then_inc(dve_order, up(dve_order))
            dve.wait_ge(dve_order, own(dve, dve_order))
            nc.vector.memset(conv_in[:, :, 0:2], 0.0).then_inc(dve_order, up(dve_order))
            dve.wait_ge(dve_order, own(dve, dve_order))
            nc.vector.memset(conv_in[:, :, CP - 2:CP], 0.0).then_inc(pad_ready, up(pad_ready))
            dve.wait_ge(pad_ready, own(dve, pad_ready))
            dve.wait_ge(inputs_landed, due(dve, inputs_landed, 16 * n_inputs_a))
            norm_dve(dve, h1, TILES)
            dve.wait_ge(products_ready, due(dve, products_ready))
            nc.vector.tensor_copy(prm[:, :], ps[7][:, 0:n_params]).then_inc(products_read, up(products_read))
            dve.wait_ge(products_read, own(dve, products_read))
            dve.wait_ge(softplus_out, due(dve, softplus_out))
            STT(lgam, lgam, 0.0, tmp8, ALU.min, ALU.subtract).then_inc(dve_order, up(dve_order))
            dve.wait_ge(dve_order, own(dve, dve_order))
            for k in range(KT):
                dve.wait_ge(xnT_ready, due(dve, xnT_ready))
                TS(uT[:, k, :], ps[k][:, 0:TOKS], pc("mix_norm_g", k), None, ALU.mult).then_inc(dve_order, up(dve_order))
                dve.wait_ge(dve_order, own(dve, dve_order))
            dve.drain().then_inc(phase_ended, 1)
            dve.wait_ge(phase_ended, phase_end(dve))
            for c in range(8):
                if c % 4 == 0:
                    dve.wait_ge(proj_read, due(dve, proj_read, 5 if c == 0 else 1))
                TS(qkm[:, c, :], conv_in[:, c, 0:TOKS], pc("conv_w", c), pc("conv_b", c), ALU.mult, ALU.add).then_inc(dve_order, up(dve_order))
                dve.wait_ge(dve_order, own(dve, dve_order))
                for j in range(1, 5):
                    signal = conv_in_ready if j == 4 else dve_order
                    STT(qkm[:, c, :], conv_in[:, c, j:j + TOKS], pc("conv_w", 8 * j + c), qkm[:, c, :], ALU.mult, ALU.add).then_inc(signal, up(signal))
                    dve.wait_ge(signal, own(dve, signal))
            dve.wait_ge(proj_ready, due(dve, proj_ready))
            for d in range(2):
                TS(lf_row, ps[2 + d][0:4, 0:TOKS], bias4[:, 2 + d:3 + d], None, ALU.add).then_inc(softplus_in, up(softplus_in))
                dve.wait_ge(softplus_in, own(dve, softplus_in))
                dve.wait_ge(softplus_out, due(dve, softplus_out))
                STT(lf_row, lf_row, 0.0, em_row(d), ALU.min, ALU.subtract).then_inc(dve_order, up(dve_order))
                dve.wait_ge(dve_order, own(dve, dve_order))
                nc.vector.tensor_tensor_scan(timed(b_row, d), ones4, timed(lf_row, d), 0.0, ALU.mult, ALU.add).then_inc(dve_order, up(dve_order))
                dve.wait_ge(dve_order, own(dve, dve_order))
                STT(g_row(d), ps[d][0:4, 0:TOKS], bias4[:, d:d + 1], b_row, ALU.add, ALU.subtract).then_inc(dve_order, up(dve_order))
                dve.wait_ge(dve_order, own(dve, dve_order))
                nc.vector.tensor_tensor_scan(timed(m_row(d), d), timed(g_row(d), d), timed(g_row(d), d), 0.0, ALU.max, ALU.max).then_inc(dve_order, up(dve_order))
                dve.wait_ge(dve_order, own(dve, dve_order))
                TT(em_row(d), m_row(d), b_row, ALU.add).then_inc(softplus_in, up(softplus_in))
                dve.wait_ge(softplus_in, own(dve, softplus_in))
            dve.drain().then_inc(phase_ended, 1)
            dve.wait_ge(phase_ended, phase_end(dve))
            for i in range(8):
                kind = "q" if i < 4 else ""
                dst = (rqT if i < 4 else rkT)[:, i % 4, :]
                part = rot_part[i % 2]
                dve.wait_ge(products_ready, due(dve, products_ready))
                TT(part, ps[i][:, 0:TOKS], C["sin" + kind], ALU.mult).then_inc(dve_order, up(dve_order))
                dve.wait_ge(dve_order, own(dve, dve_order))
                dve.wait_ge(cos_done, due(dve, cos_done))
                TT(dst, dst, part, ALU.add).then_inc(dve_order, up(dve_order))
                dve.wait_ge(dve_order, own(dve, dve_order))
            dve.drain().then_inc(phase_ended, 1)
            dve.wait_ge(phase_ended, phase_end(dve))
            dve.wait_ge(products_ready, due(dve, products_ready))
            for t, (r, _) in enumerate(TILES):
                nc.vector.tensor_copy(gate_cols[:r, t, :], ps[7][:r, t * 16:t * 16 + 16]).then_inc(dve_order, up(dve_order))
                dve.wait_ge(dve_order, own(dve, dve_order))
            TS(tmp8, lgam, -1.0, None, ALU.mult).then_inc(dve_order, up(dve_order))
            dve.wait_ge(dve_order, own(dve, dve_order))

            def weigh(n):
                kind, h = JOBS[n]
                ways = range(2 if kind == "mlstm" else 1)
                if kind == "mlstm":
                    dve.wait_ge(products_ready, due(dve, products_ready))
                for d in ways:
                    for j, (r, off) in enumerate(TILES):
                        c0, c1 = reach(j, d) if kind == "mlstm" else (0, TOKS)
                        w = weights2[2 * (n % 2) + d][:r, j, c0:c1]
                        if kind == "mlstm":
                            TS(w, ps[3 + d][:r, c0:c1], gate_cols[:r, j, 4 * d + h:4 * d + h + 1], 0.0, ALU.subtract, ALU.max).then_inc(exps_asked, up(exps_asked))
                            dve.wait_ge(exps_asked, own(dve, exps_asked))
                        else:
                            back = weights2[2 * (n % 2) + 1][:r, j, :]
                            TS(w, C["pos"][:r, :], C["posj"][:r, j:j + 1], 0.0, ALU.subtract, ALU.max).then_inc(dve_order, up(dve_order))
                            dve.wait_ge(dve_order, own(dve, dve_order))
                            TS(back, C["pos"][:r, :], C["posj"][:r, j:j + 1], 0.0, ALU.subtract, ALU.min).then_inc(dve_order, up(dve_order))
                            dve.wait_ge(dve_order, own(dve, dve_order))
                            TS(w, w, lgam[:r, h:h + 1], None, ALU.mult).then_inc(dve_order, up(dve_order))
                            dve.wait_ge(dve_order, own(dve, dve_order))
                            STT(w, back, tmp8[:r, 4 + h:5 + h], w, ALU.mult, ALU.add).then_inc(exps_asked, up(exps_asked))
                            dve.wait_ge(exps_asked, own(dve, exps_asked))
                if kind == "ret":
                    dve.wait_ge(products_ready, due(dve, products_ready))
                for d in ways:
                    for j, (r, off) in enumerate(TILES):
                        c0, c1 = reach(j, d) if kind == "mlstm" else (0, TOKS)
                        w = weights2[2 * (n % 2) + d][:r, j, :]
                        dve.wait_ge(exps_ready, due(dve, exps_ready))
                        if kind == "mlstm":
                            STT(w[:, c0:c1], ps[j][:r, c0:c1], float(P) ** -0.5, w[:, c0:c1], ALU.mult, ALU.mult).then_inc(masks_asked, up(masks_asked))
                            dve.wait_ge(masks_asked, own(dve, masks_asked))
                        else:
                            TT(w[:, off:off + r], w[:, off:off + r], ident[:r, :r], ALU.add).then_inc(dve_order, up(dve_order))
                            dve.wait_ge(dve_order, own(dve, dve_order))
                            TT(w, ps[j][:r, 0:TOKS], w, ALU.mult).then_inc(weights_ready, up(weights_ready))
                            dve.wait_ge(weights_ready, own(dve, weights_ready))
                dve.drain().then_inc(products_read, up(products_read))

            def gather_heads(n):
                kind, h = JOBS[n]
                dve.wait_ge(mixed_ready, due(dve, mixed_ready))
                for i, (r, _) in enumerate(TILES):
                    dst = heads_out[:r, int(kind == "mlstm"), i, h * P:(h + 1) * P]
                    if kind == "ret":
                        nc.vector.tensor_copy(dst, ps[5][:r, i * NUM:i * NUM + P]).then_inc(dve_order, up(dve_order))
                        dve.wait_ge(dve_order, own(dve, dve_order))
                        continue
                    for d in range(2):
                        den, to = ps[5 + d][:r, i * NUM + P:(i + 1) * NUM], den2[:r, d:d + 1]
                        nc.vector.tensor_copy(to, den).then_inc(dve_order, up(dve_order))
                        dve.wait_ge(dve_order, own(dve, dve_order))
                        STT(to, to, -1.0, to, ALU.mult, ALU.max).then_inc(dve_order, up(dve_order))
                        dve.wait_ge(dve_order, own(dve, dve_order))
                        TT(to, to, gate_cols[:r, i, 8 + 4 * d + h:9 + 4 * d + h], ALU.max).then_inc(dve_order, up(dve_order))
                        dve.wait_ge(dve_order, own(dve, dve_order))
                        nc.vector.reciprocal(to, to).then_inc(dve_order, up(dve_order))
                        dve.wait_ge(dve_order, own(dve, dve_order))
                    TS(dst, ps[5][:r, i * NUM:i * NUM + P], den2[:r, 0:1], None, ALU.mult).then_inc(dve_order, up(dve_order))
                    dve.wait_ge(dve_order, own(dve, dve_order))
                    STT(dst, ps[6][:r, i * NUM:i * NUM + P], den2[:r, 1:2], dst, ALU.mult, ALU.add).then_inc(dve_order, up(dve_order))
                    dve.wait_ge(dve_order, own(dve, dve_order))
                dve.drain().then_inc(mixed_read, up(mixed_read))

            weigh(0)
            for n in range(len(JOBS)):
                if n + 1 < len(JOBS):
                    weigh(n + 1)
                gather_heads(n)
            dve.drain().then_inc(phase_ended, 1)
            dve.wait_ge(phase_ended, phase_end(dve))

            for m in range(2):
                for t, (r, _) in enumerate(TILES):
                    x = heads_out[:r, m, t, :].rearrange("p (h c) -> p h c", h=H1)
                    flat = heads_out[:r, m, t, :]
                    sq = weights2[0][:r].rearrange("p j t -> p (j t)")[:, 0:512]
                    wide = lambda s: s.unsqueeze(2).to_broadcast([r, H1, P])
                    if m == 1:
                        TT(flat, flat, mo[:r, t, :], ALU.mult).then_inc(dve_order, up(dve_order))
                        dve.wait_ge(dve_order, own(dve, dve_order))
                    nc.vector.tensor_reduce(st4[:r], x, AX_X, ALU.add).then_inc(dve_order, up(dve_order))
                    dve.wait_ge(dve_order, own(dve, dve_order))
                    TS(st4[:r], st4[:r], 1.0 / P, None, ALU.mult).then_inc(dve_order, up(dve_order))
                    dve.wait_ge(dve_order, own(dve, dve_order))
                    TT(x, x, wide(st4[:r]), ALU.subtract).then_inc(dve_order, up(dve_order))
                    dve.wait_ge(dve_order, own(dve, dve_order))
                    TT(sq, flat, flat, ALU.mult).then_inc(dve_order, up(dve_order))
                    dve.wait_ge(dve_order, own(dve, dve_order))
                    nc.vector.tensor_reduce(st4b[:r], sq.rearrange("p (h c) -> p h c", h=H1), AX_X, ALU.add).then_inc(sqrt_asked, up(sqrt_asked))
                    dve.wait_ge(sqrt_asked, own(dve, sqrt_asked))
                    dve.wait_ge(sqrt_ready, due(dve, sqrt_ready))
                    nc.vector.reciprocal(st4b[:r], st4b[:r]).then_inc(dve_order, up(dve_order))
                    dve.wait_ge(dve_order, own(dve, dve_order))
                    last = TT(x, x, wide(st4b[:r]), ALU.mult)
                    if m == 0:
                        last.then_inc(dve_order, up(dve_order))
                        dve.wait_ge(dve_order, own(dve, dve_order))
                        last = TT(flat, flat, rg[:r, t, :], ALU.mult)
                    last.then_inc(heads_normed, up(heads_normed))
                    dve.wait_ge(heads_normed, own(dve, heads_normed))
            for f in range(8):
                dve.wait_ge(xnT_ready, due(dve, xnT_ready))
                TS(yT[:, f, :], ps[f][:, 0:TOKS], pc("ret_gn_g" if f < 4 else "mlstm_gn_g", f % 4), None, ALU.mult).then_inc(xnT_read, up(xnT_read))
                dve.wait_ge(xnT_read, own(dve, xnT_read))
            dve.wait_ge(piece_used, after(w_out_pieces))
            for t, (r, _) in enumerate(TILES):
                for half in range(2):
                    cols = slice(half * BANK, (half + 1) * BANK)
                    signal = x_ready if (t, half) == (2, 1) else dve_order
                    TT(h1[:r, t, cols], h1[:r, t, cols], ps[2 * t + half][:r, :], ALU.add).then_inc(signal, up(signal))
                    dve.wait_ge(signal, own(dve, signal))
            dve.drain().then_inc(phase_ended, 1)
            dve.wait_ge(phase_ended, phase_end(dve))
            norm_dve(dve, h1, TILES, u2)
            for k in range(KT):
                dve.wait_ge(xnT_ready, due(dve, xnT_ready))
                TS(u2T[:, k, :], ps[k][:, 0:TOKS], pc("ffn_norm_g", k), None, ALU.mult).then_inc(xnT_read, up(xnT_read))
                dve.wait_ge(xnT_read, own(dve, xnT_read))
            dve.wait_ge(logits_ready, due(dve, logits_ready))
            for t, (r, _) in enumerate(TILES):
                nc.vector.tensor_copy(aff[:r, t, :], ps[0][:r, t * N_EXP:(t + 1) * N_EXP]).then_inc(dve_order, up(dve_order))
                dve.wait_ge(dve_order, own(dve, dve_order))
                nc.vector.tensor_reduce(mx3[:r, t:t + 1], aff[:r, t, :], AX_X, ALU.max).then_inc(dve_order, up(dve_order))
                dve.wait_ge(dve_order, own(dve, dve_order))
                TS(mx3[:r, t:t + 1], mx3[:r, t:t + 1], -1.0, None, ALU.mult).then_inc(exp_asked1, up(exp_asked1))
                dve.wait_ge(exp_asked1, own(dve, exp_asked1))
            for t, (r, _) in enumerate(TILES):
                dve.wait_ge(exp_ready1, due(dve, exp_ready1))
                nc.vector.reciprocal(sum3[:r, t:t + 1], sum3[:r, t:t + 1]).then_inc(dve_order, up(dve_order))
                dve.wait_ge(dve_order, own(dve, dve_order))
                TS(aff[:r, t, :], aff[:r, t, :], sum3[:r, t:t + 1], None, ALU.mult).then_inc(aff_ready, up(aff_ready))
                dve.wait_ge(aff_ready, own(dve, aff_ready))
            dve.wait_ge(affT_ready, due(dve, affT_ready))
            nc.vector.tensor_copy(affT, ps[1][0:N_EXP, 0:TOKS]).then_inc(dve_order, up(dve_order))
            dve.wait_ge(dve_order, own(dve, dve_order))
            nc.vector.tensor_copy(left, affT).then_inc(dve_order, up(dve_order))
            dve.wait_ge(dve_order, own(dve, dve_order))
            for _ in range((CAP - 1) // 8):
                nc.vector.max(top8, left).then_inc(dve_order, up(dve_order))
                dve.wait_ge(dve_order, own(dve, dve_order))
                nc.vector.match_replace(left, top8, left, -1.0).then_inc(dve_order, up(dve_order))
                dve.wait_ge(dve_order, own(dve, dve_order))
            nc.vector.max(top8, left).then_inc(dve_order, up(dve_order))
            dve.wait_ge(dve_order, own(dve, dve_order))
            least = top8[:, (CAP - 1) % 8:(CAP - 1) % 8 + 1]
            ones16 = C["ones"][0:N_EXP, 0:1].to_broadcast([N_EXP, TOKS])
            TS(chosen, affT, least, None, ALU.is_gt).then_inc(dve_order, up(dve_order))
            dve.wait_ge(dve_order, own(dve, dve_order))
            TS(tied, affT, least, None, ALU.is_equal).then_inc(dve_order, up(dve_order))
            dve.wait_ge(dve_order, own(dve, dve_order))
            nc.vector.tensor_reduce(count1, chosen, AX_X, ALU.add).then_inc(dve_order, up(dve_order))
            dve.wait_ge(dve_order, own(dve, dve_order))
            TS(count1, count1, -1.0, float(CAP), ALU.mult, ALU.add).then_inc(dve_order, up(dve_order))
            dve.wait_ge(dve_order, own(dve, dve_order))
            nc.vector.tensor_tensor_scan(slot_row, ones16, tied, 0.0, ALU.mult, ALU.add).then_inc(dve_order, up(dve_order))
            dve.wait_ge(dve_order, own(dve, dve_order))
            TS(slot_row, slot_row, count1, None, ALU.is_le).then_inc(dve_order, up(dve_order))
            dve.wait_ge(dve_order, own(dve, dve_order))
            TT(tied, tied, slot_row, ALU.mult).then_inc(dve_order, up(dve_order))
            dve.wait_ge(dve_order, own(dve, dve_order))
            TT(chosen, chosen, tied, ALU.add).then_inc(dve_order, up(dve_order))
            dve.wait_ge(dve_order, own(dve, dve_order))
            nc.vector.tensor_tensor_scan(slot_row, ones16, chosen, 0.0, ALU.mult, ALU.add).then_inc(dve_order, up(dve_order))
            dve.wait_ge(dve_order, own(dve, dve_order))
            TT(slot_row, slot_row, chosen, ALU.mult).then_inc(dve_order, up(dve_order))
            dve.wait_ge(dve_order, own(dve, dve_order))
            TS(slot_row, slot_row, -1.0, None, ALU.add).then_inc(slots_ready, up(slots_ready))
            dve.wait_ge(slots_ready, own(dve, slots_ready))
            dve.wait_ge(slotsT_ready, due(dve, slotsT_ready))
            for t, (r, _) in enumerate(TILES):
                full = [r, N_EXP, SLOT]
                nc.vector.tensor_copy(slots[:r, t, :], ps[2][:r, t * N_EXP:(t + 1) * N_EXP]).then_inc(dve_order, up(dve_order))
                dve.wait_ge(dve_order, own(dve, dve_order))
                TT(onehot[:r, t], C["iota"][:r].unsqueeze(1).to_broadcast(full), slots[:r, t].unsqueeze(2).to_broadcast(full),
                     ALU.is_equal).then_inc(dve_order, up(dve_order))
                dve.wait_ge(dve_order, own(dve, dve_order))
                TT(weighted[:r, t], onehot[:r, t], aff[:r, t].unsqueeze(2).to_broadcast(full), ALU.mult).then_inc(onehot_ready, up(onehot_ready))
                dve.wait_ge(onehot_ready, own(dve, onehot_ready))
            for i in range(PAIRS):
                dve.wait_ge(banks_filled, due(dve, banks_filled))
                nc.vector.tensor_copy(pgT[:, i, :], ps[i][:, 0:TOKS]).then_inc(banks_read, up(banks_read))
                dve.wait_ge(banks_read, own(dve, banks_read))
            for n in range(2 * KT):
                k, half = n // 2, n % 2
                dve.wait_ge(banks_filled, due(dve, banks_filled))
                TS(xsT[:, half * 8:half * 8 + 8, k, :], ps[n % 8][:, 0:8 * CAP].rearrange("p (e s) -> p e s", e=8),
                     pc("ffn_norm_g", k), None, ALU.mult).then_inc(banks_read, up(banks_read))
                dve.wait_ge(banks_read, own(dve, banks_read))
            dve.drain().then_inc(phase_ended, 1)
            dve.wait_ge(phase_ended, phase_end(dve))
            dve.drain().then_inc(phase_ended, 1)
            dve.wait_ge(phase_ended, phase_end(dve))
            with looped(dve, LOOPS, PER) as i:
                for b in range(2):
                    for c, at, n in HID_BANKS:
                        dve.wait_ge(silu_done, due(dve, silu_done))
                        TT(hid[0:CAP, at:at + n], hid[0:CAP, at:at + n], ps[c][SLOT:SLOT + CAP, 0:n], ALU.mult).then_inc(hid_done, up(hid_done))
                    for half in range(2):
                        dve.wait_ge(hidT_ready, due(dve, hidT_ready))
                        nc.vector.tensor_copy(hidT[:, half * TURNED:(half + 1) * TURNED, :],
                                                   ps[7][:, 0:TURNED * CAP].rearrange("p (f s) -> p f s", s=CAP)).then_inc(hid_turned, up(hid_turned))
            dve.wait_ge(banks_filled, due(dve, banks_filled))
            for t, (r, _) in enumerate(TILES):
                for half in range(2):
                    cols = slice(half * BANK, (half + 1) * BANK)
                    signal = x_ready if (t, half) == (2, 1) else dve_order
                    TT(h1[:r, t, cols], h1[:r, t, cols], ps[2 * t + half][:r, :], ALU.add).then_inc(signal, up(signal))
                    dve.wait_ge(signal, own(dve, signal))
            dve.drain().then_inc(phase_ended, 1)
            dve.wait_ge(phase_ended, phase_end(dve))
            dve.wait_ge(g_rows_landed, due(dve, g_rows_landed, 16))
            final_norm_dve(dve, x1, x1)
            assert phases[str(dve.engine)] == N_PHASES_1
            dve.wait_ge(mods_turned, due(dve, mods_turned, 2))
            for u in range(2):
                halves = lambda v: v.rearrange("p (g u q) -> p u g q", g=12, u=2)[:, u]
                for s in range(2):
                    last = TT(halves(mods[:, :, s]), ps[4 + u][:, 0:48].rearrange("p (g q s) -> p s g q", g=12, q=2)[:, s],
                              halves(prm[:, PCOL["ada_b_2"]:PCOL["ada_b_2"] + 48]), ALU.add)
            last.then_inc(dve_order, up(dve_order))
            dve.wait_ge(dve_order, own(dve, dve_order))
            STT(gains, mods[:, KT:2 * KT, :], 1.0,
                  prm[:, PCOL["norm_mix_g_2"]:PCOL["norm_mix_g_2"] + KT].unsqueeze(2).to_broadcast([P, KT, 2]), ALU.add, ALU.mult).then_inc(mods_ready, up(mods_ready))
            dve.wait_ge(mods_ready, own(dve, mods_ready))
            dve.wait_ge(second_landed, due(dve, second_landed, 32))
            for s, rows in ((1, c_rows), (0, x1)):
                norm_dve(dve, rows, TILES2, cn)
                for k in range(KT):
                    dve.wait_ge(xnT_ready, due(dve, xnT_ready))
                    TS((u2x_lat, u2x_ctx)[s][:, k, :], ps[k][:, 0:SEQ], gains[:, k, s:s + 1], mods[:, k, s:s + 1],
                         ALU.mult, ALU.add).then_inc(u2x_ready, up(u2x_ready))
                    dve.wait_ge(u2x_ready, own(dve, u2x_ready))
            dve.drain().then_inc(phase_ended, 1)
            dve.wait_ge(phase_ended, phase_end(dve))
            for b in gdn_in:
                nc.vector.memset(b[:, :, :, 0:2], 0.0).then_inc(dve_order, up(dve_order))
                dve.wait_ge(dve_order, own(dve, dve_order))
                last = nc.vector.memset(b[:, :, :, CP2 - 2:CP2], 0.0)
                signal = pad_ready2 if b is gdn_in[1] else dve_order
                last.then_inc(signal, up(signal))
                dve.wait_ge(signal, own(dve, signal))
            for n in range(3):
                col = (4, 8, 0)[n]
                dve.wait_ge(group_read, due(dve, group_read))
                for ct in range(4):
                    src = gdn_in[n % 2][:, ct, :, :] if n < 2 else gdn_in[0][:, ct, 1:2, :]
                    dst = ((kT, vT, qT)[n])[:, ct, :].rearrange("p (s t) -> p s t", t=SEQ)
                    w = lambda j: pc("gdn_conv_2", 12 * j + col + ct)
                    TS(dst, src[:, :, 0:SEQ], w(0), None, ALU.mult).then_inc(dve_order, up(dve_order))
                    dve.wait_ge(dve_order, own(dve, dve_order))
                    for j in range(1, 5):
                        STT(dst, src[:, :, j:j + SEQ], w(j), dst, ALU.mult, ALU.add).then_inc(dve_order, up(dve_order))
                        dve.wait_ge(dve_order, own(dve, dve_order))
                if n == 0:
                    dve.drain().then_inc(gdn_in_ready, up(gdn_in_ready))
                dve.drain().then_inc(silu_asked, up(silu_asked))
            dve.wait_ge(gates_ready, due(dve, gates_ready))
            nc.vector.tensor_copy(ab, ps[0][:, 0:64].rearrange("p (c e) -> p c e", c=4)).then_inc(dve_order, up(dve_order))
            dve.wait_ge(dve_order, own(dve, dve_order))
            dve.wait_ge(gd_landed, due(dve, gd_landed, 48))
            TT(ab[:, :, 0:8], ab[:, :, 0:8], dtb.unsqueeze(1).to_broadcast([P, 4, 8]), ALU.add).then_inc(act_asked, up(act_asked))
            dve.wait_ge(act_asked, own(dve, act_asked))
            dve.wait_ge(act_ready, due(dve, act_ready))
            STT(gcol, ab[:, :, 0:8], 0.0, tmp32, ALU.max, ALU.add).then_inc(dve_order, up(dve_order))
            dve.wait_ge(dve_order, own(dve, dve_order))
            STT(gcol, gcol, -1.0, alog.unsqueeze(1).to_broadcast([P, 4, 8]), ALU.mult, ALU.mult).then_inc(cums_ready, up(cums_ready))
            dve.wait_ge(cums_ready, own(dve, cums_ready))
            dve.wait_ge(gates_ready, due(dve, gates_ready))
            nc.vector.tensor_copy(gcum, ps[1][:, 0:32].rearrange("p (c e) -> p c e", c=4)).then_inc(act_asked, up(act_asked))
            dve.wait_ge(act_asked, own(dve, act_asked))
            dve.wait_ge(act_ready, due(dve, act_ready))
            TT(egb, egb, beta, ALU.mult).then_inc(dve_order, up(dve_order))
            dve.wait_ge(dve_order, own(dve, dve_order))
            dve.wait_ge(silu_ready, due(dve, silu_ready, 3))
            for n in range(8):
                x = kT[:, n, :] if n < 4 else qT[:, n - 4, :]
                r = rhs_flat[:, 0:TOKS2 if n < 4 else SEQ]
                TT(sq2[:, 0:x.shape[1]], x, x, ALU.mult).then_inc(squared, up(squared))
                dve.wait_ge(squared, own(dve, squared))
                dve.wait_ge(root_ready, due(dve, root_ready))
                nc.vector.reciprocal(r, r).then_inc(dve_order, up(dve_order))
                dve.wait_ge(dve_order, own(dve, dve_order))
                STT(x, r, 1.0 if n < 4 else float(P) ** -0.5, x, ALU.mult, ALU.mult).then_inc(dve_order, up(dve_order))
                dve.wait_ge(dve_order, own(dve, dve_order))
            dve.drain().then_inc(turned_read, up(turned_read))
            for c in range(4):
                dve.wait_ge(turned, due(dve, turned))
                nc.vector.tensor_copy(k_tm[:, c], ps[c][:, :].rearrange("p (h e) -> p h e", h=4)).then_inc(turned_read, up(turned_read))
                dve.wait_ge(turned_read, own(dve, turned_read))
            for c in range(4):
                dve.wait_ge(turned, due(dve, turned))
                for d in range(2):
                    TT(vb[:, d, c], ps[4 + c][:, :].rearrange("p (h e) -> p h e", h=4),
                         beta[:, c, 4 * d:4 * d + 4].unsqueeze(2).to_broadcast([P, 4, P]), ALU.mult).then_inc(dve_order, up(dve_order))
                    dve.wait_ge(dve_order, own(dve, dve_order))
            for d in range(2):
                nc.vector.memset(state[d], 0.0).then_inc(dve_order, up(dve_order))
                dve.wait_ge(dve_order, own(dve, dve_order))
            dve.drain().then_inc(phase_ended, 1)
            dve.wait_ge(phase_ended, phase_end(dve))
            for p in range(4):
                lat = p >= 2
                for d in range(2):
                    dve.wait_ge(g_products, due(dve, g_products))
                    TT(decayT[d], bank4(4 * d), per_head(gcum[:, ORDER[d][p], 4 * d:4 * d + 4]), ALU.subtract).then_inc(dve_order, up(dve_order))
                    dve.wait_ge(dve_order, own(dve, dve_order))
                    TS(decayT[d], decayT[d], 0.0, None, ALU.min).then_inc(decay_asked, up(decay_asked))
                    dve.wait_ge(decay_asked, own(dve, decay_asked))
                for d in range(2):
                    dve.wait_ge(decay_ready, due(dve, decay_ready))
                    TT(lT[d], bank4(4 * d + 2), decayT[d], ALU.mult).then_inc(dve_order, up(dve_order))
                    dve.wait_ge(dve_order, own(dve, dve_order))
                    TT(lT[d], bank4(4 * d + 1), lT[d], ALU.mult).then_inc(dve_order, up(dve_order))
                    dve.wait_ge(dve_order, own(dve, dve_order))
                    TT(xT_[d], lT[d], join_mask(0, d, True), ALU.mult).then_inc(dve_order, up(dve_order))
                    dve.wait_ge(dve_order, own(dve, dve_order))
                    if lat:
                        TT(attT[d], bank4(4 * d + 3), decayT[d], ALU.mult).then_inc(dve_order, up(dve_order))
                        dve.wait_ge(dve_order, own(dve, dve_order))
                    TT(xT_[d], ident.unsqueeze(1).to_broadcast([P, 4, P]), xT_[d], ALU.subtract).then_inc(x_ready2, up(x_ready2))
                    dve.wait_ge(x_ready2, own(dve, x_ready2))
                for d in range(2):
                    c = ORDER[d][p]
                    end = P - 1 if d == 0 else 0
                    nc.vector.tensor_copy(kdecay[d].unsqueeze(2), decayT[d][:, :, end:end + 1]).then_inc(dve_order, up(dve_order))
                    dve.wait_ge(dve_order, own(dve, dve_order))
                    TT(kd[d], k_tm[:, c], per_head(kdecay[d]), ALU.mult).then_inc(dve_order, up(dve_order))
                    dve.wait_ge(dve_order, own(dve, dve_order))
                    if lat:
                        TT(qd[d], egrow[d], qT[:, :, (c - 2) * P:(c - 1) * P], ALU.mult).then_inc(dve_order, up(dve_order))
                        dve.wait_ge(dve_order, own(dve, dve_order))
                        TT(attT[d], attT[d], C["tri_le" if d == 0 else "tri_ge"].unsqueeze(1).to_broadcast([P, 4, P]), ALU.mult).then_inc(dve_order, up(dve_order))
                        dve.wait_ge(dve_order, own(dve, dve_order))
                for i, s in enumerate(LEVELS):
                    for d in range(2):
                        dve.wait_ge(step_filled, due(dve, step_filled))
                        TT(p1[d], bank4(4 * d), join_mask(i + 1, d), ALU.mult).then_inc(step_read, up(step_read))
                        dve.wait_ge(step_read, own(dve, step_read))
                        if i == 0:
                            c = ORDER[d][p]
                            dve.wait_ge(x_turned, due(dve, x_turned))
                            TT(rhs[d], bank4(4 * d + 3), per_head(egb[:, c, 4 * d:4 * d + 4]), ALU.mult).then_inc(dve_order, up(dve_order))
                            dve.wait_ge(dve_order, own(dve, dve_order))
                            TT(rhs[d], vb[:, d, c], rhs[d], ALU.subtract).then_inc(rhs_ready, up(rhs_ready))
                            dve.wait_ge(rhs_ready, own(dve, rhs_ready))
                    for d in range(2):
                        dve.wait_ge(step_filled, due(dve, step_filled))
                        if s != LEVELS[-1]:
                            TT(xm[d], xm[d], bank4(4 * d + 1), ALU.subtract).then_inc(dve_order, up(dve_order))
                            dve.wait_ge(dve_order, own(dve, dve_order))
                        TT(xT_[d], xT_[d], bank4(4 * d + 2), ALU.subtract).then_inc(step_read, up(step_read))
                        dve.wait_ge(step_read, own(dve, step_read))
                for d in range(2):
                    c = ORDER[d][p]
                    dve.wait_ge(chunk_filled, due(dve, chunk_filled))
                    if p < 3:
                        TT(state[d], state[d], per_head(sdecay[d]), ALU.mult).then_inc(dve_order, up(dve_order))
                        dve.wait_ge(dve_order, own(dve, dve_order))
                        TT(state[d], state[d], bank4(4 * d + 3), ALU.add).then_inc(dve_order, up(dve_order))
                        dve.wait_ge(dve_order, own(dve, dve_order))
                    if lat:
                        if p == 2:
                            nc.vector.tensor_copy(oacc[:, c - 2], bank4(4 * d + 1)).then_inc(dve_order, up(dve_order))
                            dve.wait_ge(dve_order, own(dve, dve_order))
                        else:
                            TT(oacc[:, c - 2], oacc[:, c - 2], bank4(4 * d + 1), ALU.add).then_inc(dve_order, up(dve_order))
                            dve.wait_ge(dve_order, own(dve, dve_order))
                    dve.drain().then_inc(chunk_read, up(chunk_read))
            for t in range(2):
                TT(rhs[0], oacc[:, t], oacc[:, t], ALU.mult).then_inc(dve_order, up(dve_order))
                dve.wait_ge(dve_order, own(dve, dve_order))
                nc.vector.tensor_reduce(kdecay[0], rhs[0], AX_X, ALU.add).then_inc(sqrt_asked, up(sqrt_asked))
                dve.wait_ge(sqrt_asked, own(dve, sqrt_asked))
                dve.wait_ge(sqrt_ready, due(dve, sqrt_ready))
                nc.vector.reciprocal(kdecay[0], kdecay[0]).then_inc(dve_order, up(dve_order))
                dve.wait_ge(dve_order, own(dve, dve_order))
                TT(oacc[:, t], oacc[:, t], per_head(kdecay[0]), ALU.mult).then_inc(dve_order, up(dve_order))
                dve.wait_ge(dve_order, own(dve, dve_order))
                TT(oacc[:, t], oacc[:, t], zg[:, t, :].rearrange("p (h c) -> p h c", h=4), ALU.mult).then_inc(heads_normed, up(heads_normed))
                dve.wait_ge(heads_normed, own(dve, heads_normed))
            for h in range(4):
                dve.wait_ge(turned, due(dve, turned))
                TS(oaT[:, h, :], ps[h][:, 0:SEQ], pc("gdn_onorm_g_2", 0), None, ALU.mult).then_inc(dve_order, up(dve_order))
                dve.wait_ge(dve_order, own(dve, dve_order))
            dve.drain().then_inc(phase_ended, 1)
            dve.wait_ge(phase_ended, phase_end(dve))
            for b in shift_in:
                nc.vector.memset(b[:, :, :, 0:1], 0.0).then_inc(dve_order, up(dve_order))
                dve.wait_ge(dve_order, own(dve, dve_order))
                signal = pads7 if b is shift_in[1] else dve_order
                nc.vector.memset(b[:, :, :, SP2 - 1:SP2], 0.0).then_inc(signal, up(signal))
                dve.wait_ge(signal, own(dve, signal))
            for n in range(4):
                dve.wait_ge(shift_ready, due(dve, shift_ready))
                for ct in range(4 if n < 3 else 3):
                    mu = pc("rwkv_mu_2", (4, 8, 0, 12)[n] + ct)
                    if n == 3:
                        dst = (wl, al, gl)[ct]
                    else:
                        dst = (k7, vT7, r7)[n][:, ct, :]
                    streams = slice(1, 2) if n == 2 or (n == 3 and ct == 2) else slice(0, 2)
                    dst = dst.rearrange("p (s t) -> p s t", t=SEQ)
                    x = shift_in[n % 2][:, ct, streams, :]
                    tmp = t7[:, 0:dst.shape[1] * SEQ].rearrange("p (s t) -> p s t", t=SEQ)
                    TT(tmp, x[:, :, 0:SEQ], x[:, :, 2:2 + SEQ], ALU.add).then_inc(dve_order, up(dve_order))
                    dve.wait_ge(dve_order, own(dve, dve_order))
                    STT(tmp, tmp, 0.5, x[:, :, 1:1 + SEQ], ALU.mult, ALU.subtract).then_inc(dve_order, up(dve_order))
                    dve.wait_ge(dve_order, own(dve, dve_order))
                    STT(dst, tmp, mu, x[:, :, 1:1 + SEQ], ALU.mult, ALU.add).then_inc(dve_order, up(dve_order))
                    dve.wait_ge(dve_order, own(dve, dve_order))
                dve.drain().then_inc(shift_read, up(shift_read))
            dve.drain().then_inc(lo_asked, up(lo_asked))
            for q in range(4):
                TS(kk7[:, q, :], k7[:, q, :], pc("rwkv_k_k_2", q), None, ALU.mult).then_inc(dve_order, up(dve_order))
                dve.wait_ge(dve_order, own(dve, dve_order))
                TT(t7, kk7[:, q, :], kk7[:, q, :], ALU.mult).then_inc(k7_ready, up(k7_ready))
                dve.wait_ge(k7_ready, own(dve, k7_ready))
                dve.wait_ge(root7, due(dve, root7))
                nc.vector.reciprocal(t7, t7).then_inc(dve_order, up(dve_order))
                dve.wait_ge(dve_order, own(dve, dve_order))
                TT(kk7[:, q, :], kk7[:, q, :], t7, ALU.mult).then_inc(dve_order, up(dve_order))
                dve.wait_ge(dve_order, own(dve, dve_order))
            nc.vector.memset(bonus, 0.0).then_inc(dve_order, up(dve_order))
            dve.wait_ge(dve_order, own(dve, dve_order))
            nc.vector.tensor_copy(vlat7, vT7[:, :, SEQ:]).then_inc(dve_order, up(dve_order))
            dve.wait_ge(dve_order, own(dve, dve_order))
            for c in range(NC7):
                dve.wait_ge(v7_filled, due(dve, v7_filled))
                for h in range(2):
                    nc.vector.tensor_copy(v7[C7 * h:C7 * (h + 1), c],
                                            ps[c][0:C7, :].rearrange("p (q h v) -> p q h v", q=4, h=2)[:, :, h]).then_inc(dve_order, up(dve_order))
                    dve.wait_ge(dve_order, own(dve, dve_order))
            dve.drain().then_inc(phase_ended, 1)
            dve.wait_ge(phase_ended, phase_end(dve))
            ones64 = C["ones"][:, 0:C7]
            for d in range(2):
                dve.wait_ge(sig_ready, due(dve, sig_ready))
                for q in range(4):
                    for c in range(NC7):
                        t = slice(c * C7, (c + 1) * C7)
                        last = nc.vector.tensor_tensor_scan(timed(cs7[:, q, t], d), ones64, timed(al7[:, q, t], d), 0.0, ALU.mult, ALU.add)
                    last.then_inc(dve_order, up(dve_order))
                    dve.wait_ge(dve_order, own(dve, dve_order))
                    TS(kt7[:, q, :], bt7[:, q, :], 1.0, pc("rwkv_k_a_2", q), ALU.subtract, ALU.mult).then_inc(dve_order, up(dve_order))
                    dve.wait_ge(dve_order, own(dve, dve_order))
                    STT(kt7[:, q, :], kt7[:, q, :], 1.0, k7[:, q, :], ALU.add, ALU.mult).then_inc(dve_order, up(dve_order))
                    dve.wait_ge(dve_order, own(dve, dve_order))
                    STT(e7[:, q, 0:SEQ], r7[:, q, :], pc("rwkv_r_k_2", q), kt7[:, q, SEQ:], ALU.mult, ALU.mult).then_inc(k7_ready, up(k7_ready))
                    dve.wait_ge(k7_ready, own(dve, k7_ready))
                TT(bt7, bt7, kk7, ALU.mult).then_inc(dve_order, up(dve_order))
                dve.wait_ge(dve_order, own(dve, dve_order))
                TT(al7, cs7, al7, ALU.subtract).then_inc(dve_order, up(dve_order))
                dve.wait_ge(dve_order, own(dve, dve_order))
                nc.vector.tensor_copy(dmid, chunks(cs7)[:, :, :, MID]).then_inc(dve_order, up(dve_order))
                dve.wait_ge(dve_order, own(dve, dve_order))
                nc.vector.tensor_copy(dend, chunks(cs7)[:, :, :, C7 - 1 if d == 0 else 0]).then_inc(dve_order, up(dve_order))
                dve.wait_ge(dve_order, own(dve, dve_order))
                TT(dboth, dend, dmid, ALU.subtract).then_inc(dve_order, up(dve_order))
                dve.wait_ge(dve_order, own(dve, dve_order))
                for q in range(4):
                    wide_mid = dmid[:, q, :].unsqueeze(2).to_broadcast([P, NC7, C7])
                    TT(chunks(al7)[:, q], chunks(al7)[:, q], wide_mid, ALU.subtract).then_inc(dve_order, up(dve_order))
                    dve.wait_ge(dve_order, own(dve, dve_order))
                    TT(chunks(cs7)[:, q], chunks(cs7)[:, q], wide_mid, ALU.subtract).then_inc(dve_order, up(dve_order))
                    dve.wait_ge(dve_order, own(dve, dve_order))
                for q in range(4):
                    dve.wait_ge(bonus7_ready, due(dve, bonus7_ready))
                    TT(bonus[:, q, :], bonus[:, q, :], ps[q][:, 0:SEQ], ALU.add).then_inc(dve_order, up(dve_order))
                    dve.wait_ge(dve_order, own(dve, dve_order))
                dve.drain().then_inc(e7_asked, up(e7_asked))
                dve.wait_ge(e7_ready, due(dve, e7_ready))
                TT(al7, al7, kk7, ALU.mult).then_inc(dve_order, up(dve_order))
                dve.wait_ge(dve_order, own(dve, dve_order))
                TT(bt7, bt7, e7, ALU.mult).then_inc(dve_order, up(dve_order))
                dve.wait_ge(dve_order, own(dve, dve_order))
                TT(kt7, kt7, e7, ALU.mult).then_inc(dve_order, up(dve_order))
                dve.wait_ge(dve_order, own(dve, dve_order))
                TT(rt7, rt7, r7, ALU.mult).then_inc(dve_order, up(dve_order))
                dve.wait_ge(dve_order, own(dve, dve_order))
                dve.drain().then_inc(phase_ended, 1)
                dve.wait_ge(phase_ended, phase_end(dve))
                tri_in, tri_ex = (C["tri_le"], C["tri_lt"]) if d == 0 else (C["tri_ge"], C["tri_gt"])
                over4 = lambda m: m.unsqueeze(1).to_broadcast([P, 4, P])
                for n, c in enumerate(ORDER7[d]):
                    lat = c >= NCL
                    wide_c = lambda v: v[:, :, c:c + 1].to_broadcast([P, 4, C7])
                    if n == 0:
                        nc.vector.memset(s7, 0.0).then_inc(dve_order, up(dve_order))
                        dve.wait_ge(dve_order, own(dve, dve_order))
                    TT(sm7, s7, wide_c(dmid), ALU.mult).then_inc(dve_order, up(dve_order))
                    dve.wait_ge(dve_order, own(dve, dve_order))
                    dve.wait_ge(prod7, due(dve, prod7))
                    TT(lk, bank4(1), over4(tri_ex), ALU.mult).then_inc(prod7_read, up(prod7_read))
                    dve.wait_ge(prod7_read, own(dve, prod7_read))
                    dve.wait_ge(l7_ready, due(dve, l7_ready))
                    mask2 = lambda lev, tr=False: join[:, (0 if (d == 0) != tr else 7) + lev, :].unsqueeze(1).to_broadcast([P, 2, P])
                    for g in range(2):
                        TT(xx[g][:, 1], l7[:, 2 * g:2 * g + 2, :], mask2(0, True), ALU.mult).then_inc(dve_order, up(dve_order))
                        dve.wait_ge(dve_order, own(dve, dve_order))
                        TT(xx[g][:, 1], ident.unsqueeze(1).to_broadcast([P, 2, P]), xx[g][:, 1], ALU.subtract).then_inc(inv_start, up(inv_start))
                        dve.wait_ge(inv_start, own(dve, inv_start))
                    if lat:
                        TT(ark, bank4(2), over4(tri_in), ALU.mult).then_inc(dve_order, up(dve_order))
                        dve.wait_ge(dve_order, own(dve, dve_order))
                        STT(arb, bank4(3), -1.0, over4(tri_in), ALU.mult, ALU.mult).then_inc(dve_order, up(dve_order))
                        dve.wait_ge(dve_order, own(dve, dve_order))
                    two = lambda b: ps[b][:, 0:2 * P].rearrange("p (q c) -> p q c", q=2)
                    for g in range(2):
                        dve.wait_ge(inv_filled, due(dve, inv_filled))
                        nc.vector.tensor_copy(xx[g][:, 0], two(g)).then_inc(inv_read, up(inv_read))
                        dve.wait_ge(inv_read, own(dve, inv_read))
                    for i, s in enumerate(LEVELS[:-1]):
                        for g in range(2):
                            dve.wait_ge(inv_filled, due(dve, inv_filled))
                            TT(pp[g], two(g), mask2(i + 1), ALU.mult).then_inc(inv_read, up(inv_read))
                            dve.wait_ge(inv_read, own(dve, inv_read))
                        for g in range(2):
                            dve.wait_ge(inv_filled, due(dve, inv_filled))
                            flat_x = xx[g].rearrange("p m q c -> p (m q c)")
                            TT(flat_x, flat_x, ps[2 + g][:, :], ALU.subtract).then_inc(inv_read, up(inv_read))
                            dve.wait_ge(inv_read, own(dve, inv_read))
                    quarter = lambda b: ps[b][:, 0:4 * C7].rearrange("p (q v) -> p q v", q=4)
                    TT(s7, s7, wide_c(dend), ALU.mult).then_inc(dve_order, up(dve_order))
                    dve.wait_ge(dve_order, own(dve, dve_order))
                    dve.wait_ge(c7_filled, due(dve, c7_filled))
                    TT(u7t, quarter(7), wide_c(dboth), ALU.mult).then_inc(dve_order, up(dve_order))
                    dve.wait_ge(dve_order, own(dve, dve_order))
                    TT(s7, s7, u7t, ALU.add).then_inc(dve_order, up(dve_order))
                    dve.wait_ge(dve_order, own(dve, dve_order))
                    if lat:
                        dve.wait_ge(c7_filled, due(dve, c7_filled))
                        y = yacc[:, c - NCL]
                        if d == 0:
                            nc.vector.tensor_copy(y, quarter(6)).then_inc(dve_order, up(dve_order))
                            dve.wait_ge(dve_order, own(dve, dve_order))
                        else:
                            TT(y, y, quarter(6), ALU.add).then_inc(dve_order, up(dve_order))
                            dve.wait_ge(dve_order, own(dve, dve_order))
                    dve.drain().then_inc(chunk7_done, up(chunk7_done))
                dve.drain().then_inc(phase_ended, 1)
                dve.wait_ge(phase_ended, phase_end(dve))

            nc.vector.memset(yx7, 0.0).then_inc(dve_order, up(dve_order))
            dve.wait_ge(dve_order, own(dve, dve_order))
            for c in range(NCL):
                y = yacc[:, c]
                wide_v = lambda v: v.unsqueeze(2).to_broadcast([P, 4, C7])
                nc.vector.tensor_reduce(mean7, y, AX_X, ALU.add).then_inc(dve_order, up(dve_order))
                dve.wait_ge(dve_order, own(dve, dve_order))
                TS(mean7, mean7, 1.0 / C7, None, ALU.mult).then_inc(dve_order, up(dve_order))
                dve.wait_ge(dve_order, own(dve, dve_order))
                TT(y, y, wide_v(mean7), ALU.subtract).then_inc(dve_order, up(dve_order))
                dve.wait_ge(dve_order, own(dve, dve_order))
                TT(yb7, y, y, ALU.mult).then_inc(dve_order, up(dve_order))
                dve.wait_ge(dve_order, own(dve, dve_order))
                nc.vector.tensor_reduce(var7, yb7, AX_X, ALU.add).then_inc(sqrt_asked, up(sqrt_asked))
                dve.wait_ge(sqrt_asked, own(dve, sqrt_asked))
                dve.wait_ge(sqrt_ready, due(dve, sqrt_ready))
                nc.vector.reciprocal(var7, var7).then_inc(dve_order, up(dve_order))
                dve.wait_ge(dve_order, own(dve, dve_order))
                for h in range(2):
                    rows = slice(C7 * h, C7 * (h + 1))
                    ins = TT(blocks(yx7, h), y[rows], var7[rows].unsqueeze(2).to_broadcast([C7, 4, C7]), ALU.mult)
                    signal = y7_ready if h else dve_order
                    ins.then_inc(signal, up(signal))
                    dve.wait_ge(signal, own(dve, signal))
                dve.wait_ge(turned, due(dve, turned))
                for h in range(2):
                    rows = slice(C7 * h, C7 * (h + 1))
                    nc.vector.tensor_copy(yT7[rows, :, c * C7:(c + 1) * C7], bank4(c % 2)[rows, :, C7 * h:C7 * (h + 1)]).then_inc(dve_order, up(dve_order))
                    dve.wait_ge(dve_order, own(dve, dve_order))
            dve.wait_ge(gate7_ready, due(dve, gate7_ready))
            for q in range(4):
                TS(yT7[:, q, :], yT7[:, q, :], pc("rwkv_lnx_g_2", q), pc("rwkv_lnx_b_2", q), ALU.mult, ALU.add).then_inc(dve_order, up(dve_order))
                dve.wait_ge(dve_order, own(dve, dve_order))
                TT(bonus[:, q, :], bonus[:, q, :], vlat7[:, q, :], ALU.mult).then_inc(dve_order, up(dve_order))
                dve.wait_ge(dve_order, own(dve, dve_order))
                TT(yT7[:, q, :], yT7[:, q, :], bonus[:, q, :], ALU.add).then_inc(dve_order, up(dve_order))
                dve.wait_ge(dve_order, own(dve, dve_order))
                TT(obT[:, q, :].rearrange("p (r w) -> p w r", r=ROWS7), yT7[:, q, :].rearrange("p (w r) -> p w r", r=ROWS7),
                     ps[4 + q][:, 0:SEQ].rearrange("p (w r) -> p w r", r=ROWS7), ALU.mult).then_inc(dve_order, up(dve_order))
                dve.wait_ge(dve_order, own(dve, dve_order))
            dve.drain().then_inc(phase_ended, 1)
            dve.wait_ge(phase_ended, phase_end(dve))
            for n, (g, br) in enumerate(MERGE):
                dve.wait_ge(piece_used, after(merge_pieces[n][2:]))
                dve.wait_ge(sgate_ready, due(dve, sgate_ready))
                dst = merged[:, 4 * g:4 * g + 4, :] if br == 0 else term
                for b in range(2):
                    last = TT(dst[:, 2 * b:2 * b + 2, :], sgate[n % 2][:, 2 * b:2 * b + 2, :],
                              ps[4 * (n % 2) + 2 + b][:, :].rearrange("p (c t) -> p c t", c=2), ALU.mult)
                if br:
                    last.then_inc(dve_order, up(dve_order))
                    dve.wait_ge(dve_order, own(dve, dve_order))
                    last = TT(merged[:, 4 * g:4 * g + 4, :], merged[:, 4 * g:4 * g + 4, :], term, ALU.add)
                last.then_inc(merge_read, up(merge_read))
                dve.wait_ge(merge_read, own(dve, merge_read))
            dve.wait_ge(m_row_read, due(dve, m_row_read))
            dve.wait_ge(piece_used, after(w_out2_pieces))
            for t in range(2):
                for half in range(2):
                    cols = slice(half * BANK, (half + 1) * BANK)
                    v = term.rearrange("p c t -> p (c t)")[:, cols]
                    TT(v, ps[2 * t + half][:, :], mod_row[:, cols], ALU.mult).then_inc(dve_order, up(dve_order))
                    dve.wait_ge(dve_order, own(dve, dve_order))
                    TT(x1[:, t, cols], x1[:, t, cols], v, ALU.add).then_inc(dve_order, up(dve_order))
                    dve.wait_ge(dve_order, own(dve, dve_order))
            dve.drain().then_inc(phase_ended, 1)
            dve.wait_ge(phase_ended, phase_end(dve))
            STT(gains2, mods[:, 4 * KT:5 * KT, 0], 1.0, prm[:, PCOL["norm_ffn_g_2"]:PCOL["norm_ffn_g_2"] + KT], ALU.add, ALU.mult).then_inc(dve_order, up(dve_order))
            dve.wait_ge(dve_order, own(dve, dve_order))
            nc.vector.memset(zeros1, 0.0).then_inc(dve_order, up(dve_order))
            dve.wait_ge(dve_order, own(dve, dve_order))
            norm_dve(dve, x1, TILES2, xn2)
            for k in range(KT):
                dve.wait_ge(xnT_ready, due(dve, xnT_ready))
                TS(tT[:, k, :], ps[k][:, 0:SEQ], gains2[:, k:k + 1], mods[:, 3 * KT + k, 0:1], ALU.mult, ALU.add).then_inc(tT_ready, up(tT_ready))
                dve.wait_ge(tT_ready, own(dve, tT_ready))
            dve.wait_ge(moe_landed, due(dve, moe_landed, 80))
            dve.wait_ge(logits2_ready, due(dve, logits2_ready))
            wide_t = lambda v, n: v.unsqueeze(2).to_broadcast([P, 2, n])

            def first_of(dst, cnt, v, best, n):
                TT(dst, v, wide_t(best, n), ALU.is_equal).then_inc(dve_order, up(dve_order))
                dve.wait_ge(dve_order, own(dve, dve_order))
                for t in range(2):
                    last = nc.vector.tensor_tensor_scan(cnt[:, t, :], C["ones"][:, 0:n], dst[:, t, :], 0.0, ALU.mult, ALU.add)
                last.then_inc(dve_order, up(dve_order))
                dve.wait_ge(dve_order, own(dve, dve_order))
                TS(cnt, cnt, 1.0, None, ALU.is_equal).then_inc(dve_order, up(dve_order))
                dve.wait_ge(dve_order, own(dve, dve_order))
                TT(dst, dst, cnt, ALU.mult).then_inc(dve_order, up(dve_order))
                dve.wait_ge(dve_order, own(dve, dve_order))

            TT(logits, ps[0][:, 0:2 * LG].rearrange("p (t e) -> p t e", t=2), router_b.unsqueeze(1).to_broadcast([P, 2, LG]), ALU.add).then_inc(dve_order, up(dve_order))
            dve.wait_ge(dve_order, own(dve, dve_order))
            lgrp = logits[:, :, 0:N_GRP]
            nc.vector.tensor_reduce(gmax, lgrp, AX_X, ALU.max).then_inc(dve_order, up(dve_order))
            dve.wait_ge(dve_order, own(dve, dve_order))
            TT(gp, lgrp, wide_t(gmax, N_GRP), ALU.subtract).then_inc(e2_asked, up(e2_asked))
            dve.wait_ge(e2_asked, own(dve, e2_asked))
            dve.wait_ge(e2_ready, due(dve, e2_ready))
            nc.vector.tensor_reduce(psel, gp, AX_X, ALU.add).then_inc(dve_order, up(dve_order))
            dve.wait_ge(dve_order, own(dve, dve_order))
            nc.vector.reciprocal(psel, psel).then_inc(dve_order, up(dve_order))
            dve.wait_ge(dve_order, own(dve, dve_order))
            TT(gp, gp, wide_t(psel, N_GRP), ALU.mult).then_inc(dve_order, up(dve_order))
            dve.wait_ge(dve_order, own(dve, dve_order))
            nc.vector.tensor_reduce(psel, gp, AX_X, ALU.max).then_inc(dve_order, up(dve_order))
            dve.wait_ge(dve_order, own(dve, dve_order))
            first_of(gsel, gcnt, gp, psel, N_GRP)
            TT(comb, logits[:, :, N_GRP:LG].rearrange("p t (g e) -> p t g e", g=N_GRP),
                 gsel.unsqueeze(3).to_broadcast([P, 2, N_GRP, PER_GRP]), ALU.mult).then_inc(dve_order, up(dve_order))
            dve.wait_ge(dve_order, own(dve, dve_order))
            for t in range(2):
                last = nc.vector.tensor_reduce(ing[:, t, :], comb[:, t].rearrange("p g e -> p e g"), AX_X, ALU.add)
            last.then_inc(dve_order, up(dve_order))
            dve.wait_ge(dve_order, own(dve, dve_order))
            nc.vector.tensor_reduce(max1, ing, AX_X, ALU.max).then_inc(dve_order, up(dve_order))
            dve.wait_ge(dve_order, own(dve, dve_order))
            first_of(sel1, ecnt, ing, max1, PER_GRP)
            STT(rest, sel1, -3.0e38, ing, ALU.mult, ALU.add).then_inc(dve_order, up(dve_order))
            dve.wait_ge(dve_order, own(dve, dve_order))
            nc.vector.tensor_reduce(max2, rest, AX_X, ALU.max).then_inc(dve_order, up(dve_order))
            dve.wait_ge(dve_order, own(dve, dve_order))
            first_of(sel2, ecnt, rest, max2, PER_GRP)
            TT(wt2, max2, max1, ALU.subtract).then_inc(e2_asked, up(e2_asked))
            dve.wait_ge(e2_asked, own(dve, e2_asked))
            dve.wait_ge(e2_ready, due(dve, e2_ready))
            TS(wt1, wt2, 1.0, None, ALU.add).then_inc(dve_order, up(dve_order))
            dve.wait_ge(dve_order, own(dve, dve_order))
            nc.vector.reciprocal(wt1, wt1).then_inc(dve_order, up(dve_order))
            dve.wait_ge(dve_order, own(dve, dve_order))
            TT(wt1, wt1, psel, ALU.mult).then_inc(dve_order, up(dve_order))
            dve.wait_ge(dve_order, own(dve, dve_order))
            TT(wt2, wt2, wt1, ALU.mult).then_inc(dve_order, up(dve_order))
            dve.wait_ge(dve_order, own(dve, dve_order))
            TT(sel1, sel1, wide_t(wt1, PER_GRP), ALU.mult).then_inc(dve_order, up(dve_order))
            dve.wait_ge(dve_order, own(dve, dve_order))
            TT(sel2, sel2, wide_t(wt2, PER_GRP), ALU.mult).then_inc(dve_order, up(dve_order))
            dve.wait_ge(dve_order, own(dve, dve_order))
            TT(sel1, sel1, sel2, ALU.add).then_inc(dve_order, up(dve_order))
            dve.wait_ge(dve_order, own(dve, dve_order))
            for t in range(2):
                last = TT(comb[:, t], gsel[:, t].unsqueeze(2).to_broadcast([P, N_GRP, PER_GRP]),
                          sel1[:, t].unsqueeze(1).to_broadcast([P, N_GRP, PER_GRP]), ALU.mult)
            last.then_inc(comb_ready, up(comb_ready))
            dve.wait_ge(comb_ready, own(dve, comb_ready))
            dve.wait_ge(spread_filled, due(dve, spread_filled))
            nc.vector.tensor_copy(combT[0:N_EXP2, :], ps[1][0:N_EXP2, 0:SEQ]).then_inc(combT_read, up(combT_read))
            dve.wait_ge(combT_read, own(dve, combT_read))
            dve.wait_ge(spread_read, due(dve, spread_read, N_EXP2 // 2))

            def moe_hidden(b, n, e, i=0):
                dve.wait_ge(piece_used, 6 * i + n + 2)
                TT(upb[b], ps[5 + 2 * b][:, :].rearrange("p (f t) -> p f t", f=2),
                     combB[:, bass.ds(e, 1), :].to_broadcast([P, 2, SEQ]), ALU.mult).then_inc(dve_order, up(dve_order))
                dve.wait_ge(dve_order, own(dve, dve_order))
                dve.wait_ge(silu2_ready, due(dve, silu2_ready))
                TT(hidb[b], hidb[b], upb[b], ALU.mult).then_inc(hid2_ready, up(hid2_ready))

            moe_hidden(0, moe_first, 0)
            with looped(dve, MOE_LOOPS, PER2) as i:
                moe_hidden(1, LOOP0, 2 * i + 1, i)
                moe_hidden(0, LOOP0 + 3, 2 * i + 2, i)
            moe_hidden(1, TAIL, N_EXP2 - 1)
            dve.wait_ge(m_row_filled, due(dve, m_row_filled, 3))
            dve.wait_ge(m5_ready, due(dve, m5_ready))
            for t in range(2):
                for half in range(2):
                    cols = slice(half * BANK, (half + 1) * BANK)
                    v = upb[t].rearrange("p f t -> p (f t)")
                    TT(v, ps[2 * t + half][:, :], m5_row[:, cols], ALU.mult).then_inc(dve_order, up(dve_order))
                    dve.wait_ge(dve_order, own(dve, dve_order))
                    signal = summed_ready if t and half else dve_order
                    TT(x1[:, t, cols], x1[:, t, cols], v, ALU.add).then_inc(signal, up(signal))
                    dve.wait_ge(signal, own(dve, signal))
            norm_dve(dve, x1, TILES2, xn2)
            for t in range(2):
                TT(xn2[:, t, :], xn2[:, t, :], g_out, ALU.mult).then_inc(out_ready, up(out_ready))
                dve.wait_ge(out_ready, own(dve, out_ready))

        @block.tensor
        def _(pe):
            pe.wait_ge(inputs_landed, due(pe, inputs_landed, 16 * n_inputs_a))
            for i, batch in enumerate(PARAMS):
                n = sum(m for _, m in batch)
                at = PCOL[batch[0][0]]
                last = nc.tensor.transpose(ps[7][:, at:at + n], prm_rows[i][0:n, :], ident[:n, :n])
            last.then_inc(products_ready, up(products_ready))
            pe.wait_ge(products_read, due(pe, products_read))
            transposed_norm_pe(pe, TILES)
            pe.drain().then_inc(phase_ended, 1)
            pe.wait_ge(phase_ended, phase_end(pe))
            for g in range(8):
                if g >= 2:
                    pe.wait_ge(proj_read, due(pe, proj_read))
                if g in (0, 1, 4, 5):
                    by_feature(pe, 4 * (g % 2), proj_pieces[g], uT, TOKS)
                else:
                    by_token(pe, 4 * (g % 2), proj_pieces[g], uT, TILES)
            pe.wait_ge(proj_read, due(pe, proj_read))
            for q in range(4):
                for k in range(KT):
                    last = mm(ps[q][0:4, 0:TOKS], wgate1[:, k, 4 * q:4 * q + 4], uT[:, k, :], start=k == 0, stop=k == KT - 1)
            last.then_inc(proj_ready, up(proj_ready))
            pe.drain().then_inc(phase_ended, 1)
            pe.wait_ge(phase_ended, phase_end(pe))
            for i in range(8):
                mm(ps[i][:, 0:TOKS], C["rot"], rot_in[:, i, :], start=True, stop=True).then_inc(products_ready, up(products_ready))
            pe.drain().then_inc(phase_ended, 1)
            pe.wait_ge(phase_ended, phase_end(pe))
            for t, (r, off) in enumerate(TILES):
                for q in range(4):
                    row = (g_row if q < 2 else em_row)(q % 2)
                    last = nc.tensor.transpose(ps[7][:r, t * 16 + q * 4:t * 16 + q * 4 + 4], row[:, off:off + r], ident[:4, :4])
            last.then_inc(products_ready, up(products_ready))

            def products(n):
                kind, h = JOBS[n]
                k, q = (qkm[:, 4 + h, :], qkm[:, h, :]) if kind == "mlstm" else (rkT[:, h, :], rqT[:, h, :])
                if n >= 1:
                    pe.wait_ge(products_read, due(pe, products_read))
                for j, (r, off) in enumerate(TILES):
                    last = mm(ps[j][:r, 0:TOKS], k[:, off:off + r], q, start=True, stop=True)
                if kind == "mlstm":
                    for d in range(2):
                        last = mm(ps[3 + d][:, 0:TOKS], ident[0:4, h:h + 1].to_broadcast([4, P]), m_row(d), start=True, stop=True)
                last.then_inc(products_ready, up(products_ready))

            def mix(n):
                kind, h = JOBS[n]
                if n >= 1:
                    pe.wait_ge(mixed_read, due(pe, mixed_read))
                pe.wait_ge(masks_done if kind == "mlstm" else weights_ready, due(pe, masks_done if kind == "mlstm" else weights_ready, 6 if kind == "mlstm" else 3))
                for d in range(2 if kind == "mlstm" else 1):
                    for i, (ri, oi) in enumerate(TILES):
                        js = [j for j in range(3) if kind == "ret" or (j <= i if d == 0 else j >= i)]
                        for j in js:
                            rj = TILES[j][0]
                            w = weights2[2 * (n % 2) + d][:rj, j, oi:oi + ri]
                            v = mv[:rj, j, h, :] if kind == "mlstm" else rv[:rj, j, h * P:(h + 1) * P]
                            last = mm(ps[5 + d][:ri, i * NUM:i * NUM + v.shape[1]], w, v, start=j == js[0], stop=j == js[-1])
                last.then_inc(mixed_ready, up(mixed_ready))

            def modulations(n):
                pe.wait_ge(sT_ready if n == 0 else ada_copied, due(pe, sT_ready if n == 0 else ada_copied))
                for g in (2 * n, 2 * n + 1):
                    for half, (w, slot, count, _) in enumerate(ada_pieces[g]):
                        pe.wait_ge(slot, count)
                        for k in range(4):
                            for u in range(2):
                                last = mm(ps[7][64 * u:64 * u + 2, g % 2 * SEQ:(g % 2 + 1) * SEQ], sT[:, 4 * half + k, :],
                                          w[:, k, u * SEQ:(u + 1) * SEQ], start=half + k == 0, stop=half == 1 and k == 3)
                        last.then_inc(piece_used, up(piece_used))

            products(0)
            for n in range(len(JOBS)):
                if n + 1 < len(JOBS):
                    products(n + 1)
                mix(n)
                if n < ADA_STEPS:
                    modulations(n)
            pe.drain().then_inc(phase_ended, 1)
            pe.wait_ge(phase_ended, phase_end(pe))
            pe.wait_ge(heads_normed, due(pe, heads_normed, 6))
            for f in range(8):
                for t, (r, off) in enumerate(TILES):
                    last = nc.tensor.transpose(ps[f][:, off:off + r], heads_out[:r, f // 4, t, (f % 4) * P:(f % 4 + 1) * P],
                                               ident[:r, :r])
                last.then_inc(xnT_ready, up(xnT_ready))
            pe.wait_ge(xnT_read, due(pe, xnT_read, 8))
            rows_product(pe, w_out_pieces, yT, TILES)
            pe.drain().then_inc(phase_ended, 1)
            pe.wait_ge(phase_ended, phase_end(pe))
            transposed_norm_pe(pe, TILES, u2)
            pe.wait_ge(xnT_read, due(pe, xnT_read, KT))
            pe.wait_ge(router_landed, due(pe, router_landed, 16))
            for t, (r, off) in enumerate(TILES):
                for k in range(KT):
                    last = mm(ps[0][:r, t * N_EXP:(t + 1) * N_EXP], u2T[:, k, off:off + r], w_router_sb[:, k, :],
                              start=k == 0, stop=k == KT - 1)
            last.then_inc(logits_ready, up(logits_ready))
            pe.wait_ge(aff_ready, due(pe, aff_ready, 3))
            for t, (r, off) in enumerate(TILES):
                last = nc.tensor.transpose(ps[1][0:N_EXP, off:off + r], aff[:r, t, :], ident[:r, :r])
            last.then_inc(affT_ready, up(affT_ready))
            pe.wait_ge(slots_ready, due(pe, slots_ready))
            for t, (r, off) in enumerate(TILES):
                last = nc.tensor.transpose(ps[2][:r, t * N_EXP:(t + 1) * N_EXP], slot_row[:, off:off + r], ident[:N_EXP, :N_EXP])
            last.then_inc(slotsT_ready, up(slotsT_ready))
            pe.wait_ge(onehot_ready, due(pe, onehot_ready, 3))
            for i in range(PAIRS):
                for t, (r, off) in enumerate(TILES):
                    last = nc.tensor.transpose(ps[i][:, off:off + r],
                                               weighted[:r, t].rearrange("p e s -> p (e s)")[:, i * P:(i + 1) * P], ident[:r, :r])
                last.then_inc(banks_filled, up(banks_filled))
            for n in range(2 * KT):
                k, half = n // 2, n % 2
                pe.wait_ge(banks_read, due(pe, banks_read))
                for t, (r, _) in enumerate(TILES):
                    last = mm(ps[n % 8][:, 0:8 * CAP], u2[:r, t, k * P:(k + 1) * P], onehot[:r, t, half * 8:half * 8 + 8, 0:CAP],
                              start=t == 0, stop=t == 2)
                last.then_inc(banks_filled, up(banks_filled))
            pe.drain().then_inc(phase_ended, 1)
            pe.wait_ge(phase_ended, phase_end(pe))
            pe.drain().then_inc(phase_ended, 1)
            pe.wait_ge(phase_ended, phase_end(pe))
            with looped(pe, LOOPS, PER) as i:
                def wait_piece(b, j):
                    k, count, _ = loop_pieces[b * EXPERT_PIECES + j]
                    pe.wait_ge(landed[k], i * SLOT_STEP + count)
                    return ring[:, k * PIECE:(k + 1) * PIECE]

                for b in range(2):
                    pe.wait_ge(x_cur_ready, due(pe, x_cur_ready))
                    for k in range(KT):
                        wg, wu = wait_piece(b, 2 * k), wait_piece(b, 2 * k + 1)
                        for c, at, n in HID_BANKS:
                            for row, w in ((0, wg), (SLOT, wu)):
                                last = mm(ps[c][row:row + CAP, 0:n], x_cur[b][:, k, :], w[:, at:at + n],
                                          start=k == 0, stop=k == KT - 1)
                                if c == 5:
                                    last.then_inc(piece_used, up(piece_used))
                                elif k == KT - 1 and row == SLOT:
                                    last.then_inc(gate_done, up(gate_done))
                    for half in range(2):
                        pe.wait_ge(hid_done, due(pe, hid_done, 3))
                        if half == 1:
                            pe.wait_ge(hid_turned, due(pe, hid_turned))
                        for f in range(TURNED):
                            g = half * TURNED + f
                            last = mm(ps[7][:, f * CAP:(f + 1) * CAP], hid[0:CAP, g * P:(g + 1) * P], ident[:CAP, :CAP],
                                      start=True, stop=True)
                        last.then_inc(hidT_ready, up(hidT_ready))
                    pe.wait_ge(hid_turned, due(pe, hid_turned))
                    pe.wait_ge(y_read, due(pe, y_read))
                    for j in range(FT // 2):
                        w = wait_piece(b, 2 * KT + j)
                        for f in range(2):
                            for row in (0, SLOT):
                                at = f * D + (row // SLOT) * BANK
                                last = mm(ps[6][row:row + CAP, :], hidT[:, 2 * j + f, :], w[:, at:at + BANK],
                                          start=j + f == 0, stop=j == FT // 2 - 1 and f == 1)
                        last.then_inc(piece_used, up(piece_used))
            pe.wait_ge(y_read, due(pe, y_read))
            pe.wait_ge(x_cur_ready, due(pe, x_cur_ready, 2))
            for n in range(PAIRS):
                for t, (r, off) in enumerate(TILES):
                    for half in range(2):
                        last = mm(ps[2 * t + half][:r, :], pgT[:, n, off:off + r], y_all[:, n, half * BANK:(half + 1) * BANK],
                                  start=n == 0, stop=n == PAIRS - 1)
            last.then_inc(banks_filled, up(banks_filled))
            pe.drain().then_inc(phase_ended, 1)
            pe.wait_ge(phase_ended, phase_end(pe))
            pe.wait_ge(xn_ready, due(pe, xn_ready))

            pe.wait_ge(ada_copied, due(pe, ada_copied))
            for u in range(2):
                rows = slice(64 * u, 64 * u + 2)
                for g in range(12):
                    for q in range(2):
                        at = 4 * g + 2 * q
                        last = nc.tensor.transpose(ps[4 + u][:, at:at + 2], ada_rows[rows, g, q * P:(q + 1) * P], ident[rows, rows])
                last.then_inc(mods_turned, up(mods_turned))
            for s in (1, 0):
                if s == 0:
                    pe.wait_ge(u2x_ready, due(pe, u2x_ready, 8))
                transposed_norm_pe(pe, TILES2, cn)
            pe.drain().then_inc(phase_ended, 1)
            pe.wait_ge(phase_ended, phase_end(pe))
            for n in range(4):
                base = 4 * (n % 2)
                if n >= 2:
                    pe.wait_ge(group_read, due(pe, group_read))
                if n < 3:
                    by_feature(pe, base, gdn_pieces[n], u2x_both if n < 2 else u2x_lat, TOKS2 if n < 2 else SEQ)
                else:
                    by_token(pe, base, gdn_pieces[n], u2x_lat, TILES2)
            pe.wait_ge(gd_landed, due(pe, gd_landed, 48))
            pe.wait_ge(group_read, due(pe, group_read))
            for c in range(4):
                for k in range(KT):
                    last = mm(ps[0][:, c * 16:(c + 1) * 16], (u2x_ctx if c < 2 else u2x_lat)[:, k, c % 2 * P:(c % 2 + 1) * P], wab[:, k, :], start=k == 0, stop=k == KT - 1)
            last.then_inc(gates_ready, up(gates_ready))
            pe.wait_ge(group_read, due(pe, group_read))
            pe.wait_ge(cums_ready, due(pe, cums_ready))
            for c in range(4):
                for d in range(2):
                    last = mm(ps[1][:, c * 8 + 4 * d:c * 8 + 4 * d + 4], C["tri_le" if d == 0 else "tri_ge"],
                              gcol[:, c, 4 * d:4 * d + 4], start=True, stop=True)
            last.then_inc(gates_ready, up(gates_ready))
            for n in range(8):
                pe.wait_ge(squared, due(pe, squared))
                last = mm(ps[2 + n % 2][:, 0:TOKS2 if n < 4 else SEQ], C["ones"], sq2[:, 0:TOKS2 if n < 4 else SEQ], start=True, stop=True)
                last.then_inc(normed_sum, up(normed_sum))
            pe.wait_ge(turned_read, due(pe, turned_read))
            for m, src in enumerate((kT, vT)):
                for c in range(4):
                    if m == 1 or c >= 4:
                        pe.wait_ge(turned_read, due(pe, turned_read))
                    b = 4 * m + c
                    for h in range(4):
                        last = nc.tensor.transpose(ps[b][:, h * P:(h + 1) * P], src[:, h, c * P:(c + 1) * P], ident)
                    last.then_inc(turned, up(turned))
            pe.drain().then_inc(phase_ended, 1)
            pe.wait_ge(phase_ended, phase_end(pe))
            for p in range(4):
                lat = p >= 2
                for d in range(2):
                    c = ORDER[d][p]
                    toks = slice(c * P, (c + 1) * P)
                    b0 = 4 * d
                    if p:
                        pe.wait_ge(chunk_read, due(pe, chunk_read))
                    for h in range(4):
                        e = 4 * d + h
                        hs = slice(h * P, (h + 1) * P)
                        mm(ps[b0][:, hs], gcol[:, c, e:e + 1].to_broadcast([P, P]), C["tri_le" if d == 0 else "tri_ge"],
                           start=True, stop=True)
                        mm(ps[b0 + 1][:, hs], beta[:, c, e:e + 1].to_broadcast([P, P]), ident, start=True, stop=True)
                        last = mm(ps[b0 + 2][:, hs], kT[:, h, toks], kT[:, h, toks], start=True, stop=True)
                        if lat:
                            last = mm(ps[b0 + 3][:, hs], kT[:, h, toks], qT[:, h, (c - 2) * P:(c - 1) * P], start=True, stop=True)
                    last.then_inc(g_products, up(g_products))
                for d in range(2):
                    c = ORDER[d][p]
                    pe.wait_ge(x_ready2, due(pe, x_ready2))
                    for h in range(4):
                        nc.tensor.transpose(ps[4 * d + 2][:, h * P:(h + 1) * P], xT_[d][:, h, :], ident)
                    for h in range(4):
                        last = mm(ps[4 * d + 3][:, h * P:(h + 1) * P], kT[:, h, c * P:(c + 1) * P], state[d][:, h, :],
                                  start=True, stop=True)
                    last.then_inc(x_turned, up(x_turned))
                for s in LEVELS:
                    for d in range(2):
                        if s == LEVELS[0]:
                            pe.wait_ge(x_copied, due(pe, x_copied))
                        else:
                            pe.wait_ge(step_read, due(pe, step_read))
                        for h in range(4):
                            last = mm(ps[4 * d][:, h * P:(h + 1) * P], lT[d][:, h, :], xm[d][:, h, :], start=True, stop=True)
                        last.then_inc(step_filled, up(step_filled))
                    for d in range(2):
                        pe.wait_ge(step_read, due(pe, step_read))
                        for h in range(4):
                            hs = slice(h * P, (h + 1) * P)
                            if s != LEVELS[-1]:
                                mm(ps[4 * d + 1][:, hs], xT_[d][:, h, :], p1[d][:, h, :], start=True, stop=True)
                            last = mm(ps[4 * d + 2][:, hs], p1[d][:, h, :], xT_[d][:, h, :], start=True, stop=True)
                        last.then_inc(step_filled, up(step_filled))
                for d in range(2):
                    pe.wait_ge(step_read, due(pe, step_read))
                    pe.wait_ge(rhs_ready, due(pe, rhs_ready))
                    for h in range(4):
                        last = mm(ps[4 * d][:, h * P:(h + 1) * P], xT_[d][:, h, :], rhs[d][:, h, :], start=True, stop=True)
                    last.then_inc(new_filled, up(new_filled))
                for d in range(2):
                    pe.wait_ge(new_copied, due(pe, new_copied))
                    for h in range(4):
                        hs = slice(h * P, (h + 1) * P)
                        if lat:
                            mm(ps[4 * d + 1][:, hs], qd[d][:, h, :], state[d][:, h, :], start=True, stop=False)
                            last = mm(ps[4 * d + 1][:, hs], attT[d][:, h, :], vnew[d][:, h, :], start=False, stop=True)
                        if p < 3:
                            last = mm(ps[4 * d + 3][:, hs], kd[d][:, h, :], vnew[d][:, h, :], start=True, stop=True)
                    last.then_inc(chunk_filled, up(chunk_filled))
            pe.wait_ge(chunk_read, due(pe, chunk_read, 2))
            pe.wait_ge(heads_normed, due(pe, heads_normed, 2))
            for h in range(4):
                for t in range(2):
                    last = nc.tensor.transpose(ps[h][:, t * P:(t + 1) * P], oacc[:, t, h, :], ident)
                last.then_inc(turned, up(turned))
            pe.drain().then_inc(phase_ended, 1)
            pe.wait_ge(phase_ended, phase_end(pe))
            for n in range(4):
                base = 4 * (n % 2)
                if n >= 2:
                    pe.wait_ge(shift_ready, due(pe, shift_ready))
                by_feature(pe, base, rwkv_pieces[n], u2x_lat if n == 2 else u2x_both, SEQ if n == 2 else TOKS2)
            pe.wait_ge(shift_ready, due(pe, shift_ready, 2))
            for q in range(4):
                pe.wait_ge(k7_ready, due(pe, k7_ready))
                mm(ps[0][:, :], C["half_ones"], t7, start=True, stop=True).then_inc(sum7_ready, up(sum7_ready))
            pe.wait_ge(root7, due(pe, root7, 4))
            for c in range(NC7):
                for q in range(4):
                    last = mm(ps[c][0:C7, q * P:(q + 1) * P], vT7[:, q, c * C7:(c + 1) * C7], ident, start=True, stop=True)
                last.then_inc(v7_filled, up(v7_filled))
            pe.drain().then_inc(phase_ended, 1)
            pe.wait_ge(phase_ended, phase_end(pe))
            def decays_pe(d):
                ks = slice(64 * d, 64 * d + 64)
                pe.wait_ge(w2_landed, due(pe, w2_landed, 32))
                if d == 0:
                    pe.wait_ge(lo_ready, due(pe, lo_ready))
                for q in range(4):
                    mm(ps[q][:, :], w2sb[ks, q * P:(q + 1) * P], wl[ks, :], start=True, stop=True)
                    last = mm(ps[4 + q][:, :], a2sb[ks, q * P:(q + 1) * P], al[ks, :], start=True, stop=True)
                last.then_inc(zw_ready, up(zw_ready))
                for q in range(4):
                    pe.wait_ge(k7_ready, due(pe, k7_ready))
                    mm(ps[q][:, 0:SEQ], C["half_ones"], e7[:, q, 0:SEQ], start=True, stop=True).then_inc(bonus7_ready, up(bonus7_ready))
                pe.drain().then_inc(phase_ended, 1)
                pe.wait_ge(phase_ended, phase_end(pe))

            def invert7_pe():
                for g in range(2):
                    pe.wait_ge(inv_start, due(pe, inv_start))
                    for i in range(2):
                        last = nc.tensor.transpose(ps[g][:, i * P:(i + 1) * P], xx[g][:, 1, i, :], ident)
                    last.then_inc(inv_filled, up(inv_filled))
                for s in LEVELS[:-1]:
                    for g in range(2):
                        pe.wait_ge(inv_read, due(pe, inv_read))
                        for i in range(2):
                            last = mm(ps[g][:, i * P:(i + 1) * P], l7[:, 2 * g + i, :], xx[g][:, 0, i, :], start=True, stop=True)
                        last.then_inc(inv_filled, up(inv_filled))
                    for g in range(2):
                        pe.wait_ge(inv_read, due(pe, inv_read))
                        for i in range(2):
                            mm(ps[2 + g][:, i * P:(i + 1) * P], xx[g][:, 1, i, :], pp[g][:, i, :], start=True, stop=True)
                            last = mm(ps[2 + g][:, (2 + i) * P:(3 + i) * P], pp[g][:, i, :], xx[g][:, 1, i, :], start=True, stop=True)
                        last.then_inc(inv_filled, up(inv_filled))
                pe.wait_ge(inv_read, due(pe, inv_read, 2))

            for d in range(2):
                decays_pe(d)
                for n, c in enumerate(ORDER7[d]):
                    lat = c >= NCL
                    ax, bx, kx, rx = (v[n % 2] for v in (ax2, bx2, kx2, rx2))
                    pe.wait_ge(spread_ready, due(pe, spread_ready, 4 if lat else 3))
                    for q in range(4):
                        qs = slice(q * P, (q + 1) * P)
                        mm(ps[0][:, qs], bx[:, q, :], ax[:, q, :], start=True, stop=True)
                        last = mm(ps[1][:, qs], kx[:, q, :], ax[:, q, :], start=True, stop=True)
                        if lat:
                            mm(ps[2][:, qs], kx[:, q, :], rx[:, q, :], start=True, stop=True)
                            last = mm(ps[3][:, qs], bx[:, q, :], rx[:, q, :], start=True, stop=True)
                    last.then_inc(prod7, up(prod7))
                    if n:
                        pe.wait_ge(chunk7_done, due(pe, chunk7_done))
                    for q in range(4):
                        qs = slice(q * P, (q + 1) * P)
                        nc.tensor.transpose(ps[6][:, qs], bx[:, q, :], ident)
                        last = nc.tensor.transpose(ps[7][:, qs], kx[:, q, :], ident)
                    last.then_inc(turned7, up(turned7))
                    pe.wait_ge(prod7_read, due(pe, prod7_read))
                    for q in range(4):
                        qs = slice(q * C7, (q + 1) * C7)
                        mm(ps[4][:, qs], ax[:, q, :], sm7[:, q, :], start=True, stop=False)
                        last = mm(ps[4][:, qs], lk[:, q, :], v7[:, c, q, :], start=False, stop=True)
                    last.then_inc(u7_filled, up(u7_filled))
                    invert7_pe()
                    pe.wait_ge(u7_copied, due(pe, u7_copied))
                    for q in range(4):
                        last = mm(ps[5][:, q * C7:(q + 1) * C7], xx[q // 2][:, 1, q % 2, :], u7[:, q, :], start=True, stop=True)
                    last.then_inc(u7_filled, up(u7_filled))
                    pe.wait_ge(u7_copied, due(pe, u7_copied))
                    for q in range(4):
                        qs = slice(q * C7, (q + 1) * C7)
                        mm(ps[7][:, qs], kx[:, q, :], v7[:, c, q, :], start=True, stop=False)
                        last = mm(ps[7][:, qs], bx[:, q, :], u7[:, q, :], start=False, stop=True)
                    last.then_inc(c7_filled, up(c7_filled))
                    if lat:
                        for q in range(4):
                            qs = slice(q * C7, (q + 1) * C7)
                            mm(ps[6][:, qs], rx[:, q, :], sm7[:, q, :], start=True, stop=False)
                            mm(ps[6][:, qs], ark[:, q, :], v7[:, c, q, :], start=False, stop=False)
                            last = mm(ps[6][:, qs], arb[:, q, :], u7[:, q, :], start=False, stop=True)
                        last.then_inc(c7_filled, up(c7_filled))
                pe.wait_ge(chunk7_done, due(pe, chunk7_done))
                pe.drain().then_inc(phase_ended, 1)
                pe.wait_ge(phase_ended, phase_end(pe))
            for c in range(NCL):
                pe.wait_ge(y7_ready, due(pe, y7_ready))
                for q in range(4):
                    last = nc.tensor.transpose(ps[c % 2][:, q * P:(q + 1) * P], yx7[:, q, :], ident)
                last.then_inc(turned, up(turned))
            pe.wait_ge(g2_landed, due(pe, g2_landed, 16))
            for q in range(4):
                last = mm(ps[4 + q][:, 0:SEQ], g2sb[:, q * P:(q + 1) * P], gl, start=True, stop=True)
            last.then_inc(gate7_ready, up(gate7_ready))
            pe.drain().then_inc(phase_ended, 1)
            pe.wait_ge(phase_ended, phase_end(pe))
            def two_in_a_bank(pe, base, views, x):
                for _, slot, count, _ in views:
                    pe.wait_ge(slot, count)
                kts = views[0][0].shape[1]
                n = kts * len(views)
                for ct in range(4):
                    for k in range(n):
                        last = mm(ps[base + ct // 2][:, ct % 2 * SEQ:(ct % 2 + 1) * SEQ],
                                  views[k // kts][0][:, k % kts, ct * P:(ct + 1) * P], x[:, k, :], start=k == 0, stop=k == n - 1)
                        if ct == 3 and k % kts == kts - 1:
                            last.then_inc(piece_used, up(piece_used))

            def row_of_columns_pe(pe, base, j):
                for k in range(KT):
                    last = mm(ps[base + k // 4][:, k % 4 * P:(k % 4 + 1) * P], mods[:, j * KT + k, 0:1].to_broadcast([P, P]), ident,
                              start=True, stop=True)
                last.then_inc(m_row_filled, up(m_row_filled))

            for n, (g, br) in enumerate(MERGE):
                base = 4 * (n % 2)
                if n >= 2:
                    pe.wait_ge(merge_read, due(pe, merge_read))
                two_in_a_bank(pe, base, merge_pieces[n][:2], u2x_lat)
                two_in_a_bank(pe, base + 2, merge_pieces[n][2:], (oaT, obT)[br])
            pe.wait_ge(merge_read, due(pe, merge_read, 2))
            row_of_columns_pe(pe, 4, 2)
            rows_product(pe, w_out2_pieces, merged, TILES2)
            pe.drain().then_inc(phase_ended, 1)
            pe.wait_ge(phase_ended, phase_end(pe))
            transposed_norm_pe(pe, TILES2, xn2)
            pe.wait_ge(moe_landed, due(pe, moe_landed, 80))
            pe.wait_ge(tT_ready, due(pe, tT_ready, KT))
            for t in range(2):
                for k in range(KT):
                    last = mm(ps[0][:, t * LG:(t + 1) * LG], tT[:, k, t * P:(t + 1) * P], router_w[:, k, :], start=k == 0, stop=k == KT - 1)
            last.then_inc(logits2_ready, up(logits2_ready))
            row_of_columns_pe(pe, 2, 5)
            pe.wait_ge(comb_ready, due(pe, comb_ready))
            for t in range(2):
                last = nc.tensor.transpose(ps[1][0:N_EXP2, t * P:(t + 1) * P], comb[:, t].rearrange("p g e -> p (g e)"), ident)
            last.then_inc(spread_filled, up(spread_filled))
            pe.wait_ge(combT_read, due(pe, combT_read))
            for n in range(N_EXP2 // 2):
                if n >= 4:
                    pe.wait_ge(spread_read, due(pe, spread_read))
                for e in (2 * n, 2 * n + 1):
                    last = mm(ps[4 + n % 4][:, e % 2 * SEQ:(e % 2 + 1) * SEQ], ident[0:N_EXP2, e:e + 1].to_broadcast([N_EXP2, P]),
                              combT[0:N_EXP2, :], start=True, stop=True)
                last.then_inc(spread_filled, up(spread_filled))
            pe.wait_ge(spread_read, due(pe, spread_read, 4))
            pe.wait_ge(m5_ready, due(pe, m5_ready))
            for b in range(4):
                mm(ps[b][:, :], zeros1, x1[:, 0, 0:BANK], start=True, stop=False)

            def moe_gate_up(b, n, i=0):
                for which in range(2):
                    pe.wait_ge(landed[(n + which) % RING], 16 * i + moe_count[n + which])
                    w = moe_view(n + which).rearrange("p (k c) -> p k c", k=KT)
                    for f in range(2):
                        for k in range(KT):
                            last = mm(ps[4 + 2 * b + which][:, f * SEQ:(f + 1) * SEQ], w[:, k, f * P:(f + 1) * P], tT[:, k, :],
                                      start=k == 0, stop=k == KT - 1)
                    last.then_inc(piece_used, up(piece_used))

            def moe_down(b, n, i=0):
                pe.wait_ge(landed[n % RING], 16 * i + moe_count[n])
                pe.wait_ge(hid2_ready, due(pe, hid2_ready))
                w = moe_view(n).rearrange("p (k c) -> p k c", k=2)
                for f in range(2):
                    for t in range(2):
                        for half in range(2):
                            last = mm(ps[2 * t + half][:, :], hidb[b][:, f, t * P:(t + 1) * P], w[:, f, half * BANK:(half + 1) * BANK],
                                      start=False, stop=False)
                last.then_inc(piece_used, up(piece_used))

            moe_gate_up(0, moe_first)
            with looped(pe, MOE_LOOPS, PER2) as i:
                moe_gate_up(1, LOOP0, i)
                moe_down(0, LOOP0 + 2, i)
                moe_gate_up(0, LOOP0 + 3, i)
                moe_down(1, LOOP0 + 5, i)
            moe_gate_up(1, TAIL)
            moe_down(0, TAIL + 2)
            moe_down(1, TAIL + 3)
            for b in range(4):
                last = mm(ps[b][:, :], zeros1, x1[:, 0, 0:BANK], start=False, stop=True)
            last.then_inc(m_row_filled, up(m_row_filled))

def kernel(**inputs):
    import numpy as _np
    import concourse.bacc as _bacc
    from concourse.bass_utils import run_bass_kernel_spmd as _run

    nc = _bacc.Bacc("TRN2", target_bir_lowering=False, num_devices=1)
    arrays, args, consts = {}, {}, []
    for name, value in inputs.items():
        a = _np.ascontiguousarray(value)
        a = a.reshape(a.shape[1:]) if a.ndim > 1 and a.shape[0] == 1 else a
        arrays[f"in_{name}"] = a
        args[name] = nc.dram_tensor(f"in_{name}", a.shape, F32, kind="ExternalInput").ap()
    for i, a in enumerate(constant_arrays()):
        arrays[f"const_{i}"] = a
        consts.append(nc.dram_tensor(f"const_{i}", a.shape, F32, kind="ExternalInput").ap())
    out = nc.dram_tensor("out", (SEQ, D), F32, kind="ExternalOutput").ap()
    build(nc, args, consts, out)
    r = _run(nc, [arrays], core_ids=[0])
    return r.results[0]["out"].reshape(1, SEQ, D)
```
